# Optimizing a Trainium2 kernel written in Bass

```python
import jax, jax.numpy as jnp
from jax import lax
import numpy as np

D_MODEL = 2048
BATCH = 1
SEQ = 256
DEPTH = 1

GLA_W = 3 * D_MODEL // 8
MLSTM_W = 3 * D_MODEL // 8
SGU_W = D_MODEL - GLA_W - MLSTM_W

GLA_HEADS = 4
GLA_DV = GLA_W // GLA_HEADS
GLA_DK = GLA_DV // 2
GLA_GATE_RANK = 16
GLA_GATE_TAU = 16.0

MLSTM_HEADS = 4
MLSTM_DV = MLSTM_W // MLSTM_HEADS
MLSTM_DK = MLSTM_DV // 2
CONV_WIDTH = 4

SGU_GROUPS = 4
SGU_CH = SGU_W // SGU_GROUPS
SGU_BLOCK = 128

REC_CHUNK = 64
D_FF = -(-8 * D_MODEL // 768) * 256
EPS = 1e-6

kernel_name = "hymba_style_gla_mlstm_gmlp_hybrid"

def _proj_sizes():
    gk = GLA_HEADS * GLA_DK
    mk = MLSTM_HEADS * MLSTM_DK
    return (gk, gk, GLA_W, GLA_W, GLA_GATE_RANK,
            mk, mk, MLSTM_W, MLSTM_W, MLSTM_HEADS, MLSTM_HEADS,
            SGU_W, SGU_W)

def rms_norm(x, g):
    xf = x.astype(jnp.float32)
    y = xf * lax.rsqrt(jnp.mean(xf * xf, axis=-1, keepdims=True) + EPS)
    return (y * g.astype(jnp.float32)).astype(x.dtype)

def to_chunks(t, c):
    b, s, h, d = t.shape
    return t.reshape(b, s // c, c, h, d).transpose(1, 0, 3, 2, 4)

def from_chunks(t):
    n, b, h, c, d = t.shape
    return t.transpose(1, 0, 3, 2, 4).reshape(b, n * c, h, d)

def gla_chunked(q, k, v, log_a):
    b, s, h, dk = q.shape
    dv = v.shape[-1]
    mask = jnp.tril(jnp.ones((REC_CHUNK, REC_CHUNK), dtype=bool))

    def step(state, inp):
        qb, kb, vb, ab = inp
        cum = jnp.cumsum(ab, axis=2)
        diff = cum[:, :, :, None, :] - cum[:, :, None, :, :]
        decay = jnp.exp(jnp.where(mask[:, :, None], diff, -jnp.inf))
        attn = jnp.einsum('bhtsd,bhsd->bhts', qb[:, :, :, None, :] * decay, kb)
        o = (jnp.einsum('bhts,bhsv->bhtv', attn, vb)
             + jnp.einsum('bhtd,bhdv->bhtv', qb * jnp.exp(cum), state))
        last = cum[:, :, -1:, :]
        k_dec = kb * jnp.exp(last - cum)
        state = state * jnp.exp(last[:, :, 0, :, None]) + jnp.einsum('bhsd,bhsv->bhdv', k_dec, vb)
        return state, o

    s0 = jnp.zeros((b, h, dk, dv), jnp.float32)
    _, o = lax.scan(step, s0, tuple(to_chunks(t, REC_CHUNK) for t in (q, k, v, log_a)))
    return from_chunks(o)

def mlstm_chunked(q, k, v, i_pre, log_f):
    b, s, h, dk = q.shape
    dv = v.shape[-1]
    n = s // REC_CHUNK
    mask = jnp.tril(jnp.ones((REC_CHUNK, REC_CHUNK), dtype=bool))
    gate_chunks = lambda g: g.reshape(b, n, REC_CHUNK, h).transpose(1, 0, 3, 2)

    def step(carry, inp):
        c_st, n_st, m_st = carry
        qb, kb, vb, ib, fb = inp
        cum = jnp.cumsum(fb, axis=-1)
        dmat = jnp.where(mask, cum[..., :, None] - cum[..., None, :] + ib[..., None, :], -jnp.inf)
        inter = cum + m_st[..., None]
        m_t = jnp.maximum(inter, jnp.max(dmat, axis=-1))
        w = jnp.exp(dmat - m_t[..., None])
        sc_inter = jnp.exp(inter - m_t)
        sc = jnp.einsum('bhtd,bhsd->bhts', qb, kb) * w
        num = (jnp.einsum('bhts,bhsv->bhtv', sc, vb)
               + sc_inter[..., None] * jnp.einsum('bhtd,bhdv->bhtv', qb, c_st))
        den = jnp.sum(sc, axis=-1) + sc_inter * jnp.einsum('bhtd,bhd->bht', qb, n_st)
        h_out = num / jnp.maximum(jnp.abs(den), jnp.exp(-m_t))[..., None]
        total = cum[..., -1]
        g = total[..., None] - cum + ib
        m_new = jnp.maximum(total + m_st, jnp.max(g, axis=-1))
        wj = jnp.exp(g - m_new[..., None])
        dprev = jnp.exp(total + m_st - m_new)
        c_new = dprev[..., None, None] * c_st + jnp.einsum('bhs,bhsd,bhsv->bhdv', wj, kb, vb)
        n_new = dprev[..., None] * n_st + jnp.einsum('bhs,bhsd->bhd', wj, kb)
        return (c_new, n_new, m_new), h_out

    init = (jnp.zeros((b, h, dk, dv), jnp.float32),
            jnp.zeros((b, h, dk), jnp.float32),
            jnp.zeros((b, h), jnp.float32))
    xs = (to_chunks(q, REC_CHUNK), to_chunks(k, REC_CHUNK), to_chunks(v, REC_CHUNK),
          gate_chunks(i_pre), gate_chunks(log_f))
    _, hs = lax.scan(step, init, xs)
    return from_chunks(hs)

def causal_dwconv(x, w):
    kw = w.shape[0]
    s = x.shape[1]
    xp = jnp.pad(x, ((0, 0), (kw - 1, 0), (0, 0)))
    return sum(xp[:, j:j + s] * w[j] for j in range(kw))

def spatial_gating(u, v, w_s, b_s, ln_g, ln_b):
    b, s, _ = v.shape
    vf = v.astype(jnp.float32)
    mu = jnp.mean(vf, axis=-1, keepdims=True)
    var = jnp.mean(jnp.square(vf - mu), axis=-1, keepdims=True)
    vn = ((vf - mu) * lax.rsqrt(var + EPS) * ln_g + ln_b).astype(v.dtype)
    vb = vn.reshape(b, s // SGU_BLOCK, SGU_BLOCK, SGU_GROUPS, SGU_CH)
    w_causal = jnp.tril(w_s)
    mixed = jnp.einsum('gts,bnsgc->bntgc', w_causal, vb) + b_s.T[None, None, :, :, None]
    return u * mixed.reshape(b, s, SGU_W)

def hybrid_layer(x, norm_mix, w_in, gla_a2, gla_ab, gla_norm, ml_conv, ml_ib, ml_fb, ml_norm,
                 sgu_ln_g, sgu_ln_b, sgu_w, sgu_b, w_out, norm_ffn, w_gu, w_down):
    f32 = jnp.float32
    b, s, _ = x.shape
    h = rms_norm(x, norm_mix)
    proj = h @ w_in
    idx = np.cumsum(_proj_sizes())[:-1].tolist()
    (gq, gk, gv, gg, ga1, mq, mk, mv, mo, mi, mf, su, sv) = jnp.split(proj, idx, axis=-1)

    q = gq.reshape(b, s, GLA_HEADS, GLA_DK).astype(f32) * (GLA_DK ** -0.5)
    k = gk.reshape(b, s, GLA_HEADS, GLA_DK).astype(f32)
    v = gv.reshape(b, s, GLA_HEADS, GLA_DV).astype(f32)
    log_a = jax.nn.log_sigmoid((ga1 @ gla_a2 + gla_ab).astype(f32)) / GLA_GATE_TAU
    log_a = log_a.reshape(b, s, GLA_HEADS, GLA_DK)
    o_gla = gla_chunked(q, k, v, log_a)
    o_gla = rms_norm(o_gla, gla_norm.reshape(GLA_HEADS, GLA_DV)).reshape(b, s, GLA_W)
    out_a = o_gla * jax.nn.silu(gg.astype(f32))

    mqk = jax.nn.silu(causal_dwconv(jnp.concatenate([mq, mk], axis=-1), ml_conv))
    mq2, mk2 = jnp.split(mqk, 2, axis=-1)
    qm = mq2.reshape(b, s, MLSTM_HEADS, MLSTM_DK).astype(f32)
    km = mk2.reshape(b, s, MLSTM_HEADS, MLSTM_DK).astype(f32) * (MLSTM_DK ** -0.5)
    vm = mv.reshape(b, s, MLSTM_HEADS, MLSTM_DV).astype(f32)
    i_pre = (mi + ml_ib).astype(f32)
    log_f = jax.nn.log_sigmoid((mf + ml_fb).astype(f32))
    o_ml = mlstm_chunked(qm, km, vm, i_pre, log_f)
    o_ml = rms_norm(o_ml, ml_norm.reshape(MLSTM_HEADS, MLSTM_DV)).reshape(b, s, MLSTM_W)
    out_b = o_ml * jax.nn.sigmoid(mo.astype(f32))

    out_c = spatial_gating(jax.nn.gelu(su), jax.nn.gelu(sv), sgu_w, sgu_b, sgu_ln_g, sgu_ln_b)

    mix = jnp.concatenate([out_a.astype(x.dtype), out_b.astype(x.dtype), out_c.astype(x.dtype)], axis=-1)
    x = x + mix @ w_out

    hf = rms_norm(x, norm_ffn)
    gate, up = jnp.split(hf @ w_gu, 2, axis=-1)
    return x + (jax.nn.silu(gate) * up) @ w_down

def setup_inputs(seed: int = 0) -> dict:
    key = jax.random.key(seed)
    ks = jax.random.split(key, 20)
    L, D = DEPTH, D_MODEL
    nrm = lambda k, shape, scale: jax.random.normal(k, shape, jnp.float32) * scale
    p = sum(_proj_sizes())
    gk = GLA_HEADS * GLA_DK
    mk = MLSTM_HEADS * MLSTM_DK
    return {
        "x": nrm(ks[0], (BATCH, SEQ, D), 1.0),
        "norm_mix": 1.0 + nrm(ks[1], (L, D), 0.1),
        "w_in": nrm(ks[2], (L, D, p), D ** -0.5),
        "gla_a2": nrm(ks[3], (L, GLA_GATE_RANK, gk), GLA_GATE_RANK ** -0.5),
        "gla_ab": nrm(ks[4], (L, gk), 0.1),
        "gla_norm": 1.0 + nrm(ks[5], (L, GLA_W), 0.1),
        "ml_conv": nrm(ks[6], (L, CONV_WIDTH, 2 * mk), CONV_WIDTH ** -0.5),
        "ml_ib": nrm(ks[7], (L, MLSTM_HEADS), 0.1),
        "ml_fb": 3.0 + 3.0 * jax.random.uniform(ks[8], (L, MLSTM_HEADS), jnp.float32),
        "ml_norm": 1.0 + nrm(ks[9], (L, MLSTM_W), 0.1),
        "sgu_ln_g": 1.0 + nrm(ks[10], (L, SGU_W), 0.1),
        "sgu_ln_b": nrm(ks[11], (L, SGU_W), 0.1),
        "sgu_w": nrm(ks[12], (L, SGU_GROUPS, SGU_BLOCK, SGU_BLOCK), SGU_BLOCK ** -0.5),
        "sgu_b": 1.0 + nrm(ks[13], (L, SGU_GROUPS, SGU_BLOCK), 0.1),
        "w_out": nrm(ks[14], (L, D, D), D ** -0.5),
        "norm_ffn": 1.0 + nrm(ks[15], (L, D), 0.1),
        "w_gu": nrm(ks[16], (L, D, 2 * D_FF), D ** -0.5),
        "w_down": nrm(ks[17], (L, D_FF, D), D_FF ** -0.5),
        "norm_final": 1.0 + nrm(ks[18], (D,), 0.1),
    }

def reference(x, norm_mix, w_in, gla_a2, gla_ab, gla_norm, ml_conv, ml_ib, ml_fb, ml_norm,
              sgu_ln_g, sgu_ln_b, sgu_w, sgu_b, w_out, norm_ffn, w_gu, w_down, norm_final):
    for l in range(DEPTH):
        x = hybrid_layer(x, norm_mix[l], w_in[l], gla_a2[l], gla_ab[l], gla_norm[l],
                         ml_conv[l], ml_ib[l], ml_fb[l], ml_norm[l],
                         sgu_ln_g[l], sgu_ln_b[l], sgu_w[l], sgu_b[l],
                         w_out[l], norm_ffn[l], w_gu[l], w_down[l])
    return rms_norm(x, norm_final)


_drawn_inputs = setup_inputs


def setup_inputs(seed=0):
    import zlib

    import numpy as np

    out = dict(_drawn_inputs(seed))
    spreads = {}
    factors = {'gla_ab': 3.929, 'ml_ib': 64.0, 'sgu_ln_b': 2.737}
    for name, (base, spread) in spreads.items():
        noise = np.random.default_rng([zlib.crc32(name.encode()), seed]).standard_normal(out[name].shape)
        drawn = base * np.exp(spread * noise) if base else spread * noise
        out[name] = __import__('jax').numpy.asarray(drawn.astype(out[name].dtype))
    for name, factor in factors.items():
        out[name] = (out[name] * factor).astype(out[name].dtype)
    return out
```

```python
from contextlib import ExitStack

import concourse.bass as bass
from concourse import mybir

F32 = mybir.dt.float32
F32R = mybir.dt.float32r
I8 = mybir.dt.int8
ALU = mybir.AluOpType
ACT = mybir.ActivationFunctionType
AX_X = mybir.AxisListType.X

P = 128
D = 2048
T = 256
NB = T // P
H = 4
DV = 192
DK = 96
AW = H * DV
CW = D - 2 * AW
RANK = 16
TAU = 16.0
FF = 5632
EPS = 1e-6
KC = D // P
FC = FF // P
GW = 512
UC = 2
R = 4
GELU_C1 = 0.044715
GELU_C0 = 0.7978845608028654

GQ, GK, GV, GG, GA1 = 0, 384, 768, 1536, 2304
MQ, MK, MV, MO, MI, MF = 2320, 2704, 3088, 3856, 4624, 4628
SU, SV = 4632, 5144
IN_GROUPS = [(GQ, GW, 0), (GW, GW, GW), (2048, 272, 2048), (1024, GW, 1024), (1536, GW, 1536),
             (MQ, GW, MQ), (MQ + GW, GW, MQ + GW), (MO + GW, 264, MO + GW),
             (SV, GW, 0), (SU, GW, MQ), (MQ + 1024, GW, MQ + 1024), (MO, GW, MO)]
TOKW = 4632
UPG = KC // UC
UPD = FC // UC
NG_IN, NG_OUT, NG_FF, NG_DN = len(IN_GROUPS), D // GW, FF // GW, D // GW
U_OUT = NG_IN * UPG
U_FF = U_OUT + NG_OUT * UPG
U_DN = U_FF + NG_FF * 2 * UPG
MIX_A, MIX_C, MIX_B = [0, 1, 2], [6, 7], [3, 4, 5]
LEVEL_AT, AT_O_A, AT_OT_A = 38, 70, 76
AT_IF, AT_RAW, AT_CONV, AT_MB = 78, 83, 88, 91
AT_GELU, AT_MIXED, AT_OT_C = 84, 90, 95
AT_SC, AT_O_B, AT_OT_B, AT_MO = 97, 100, 103, 100
MIXED_A, MIXED_C, MIXED_B = 6, 10, 16
OUT_ORDER = [(n, k) for n in (0, 1) for k in MIX_A + MIX_C] + [(n, k) for n in (0, 1) for k in MIX_B] \
    + [(n, k) for n in (2, 3) for k in range(UPG)]

OUT_DONE = [U_OUT + max(i for i, (m, _k) in enumerate(OUT_ORDER) if m == n) + 1 for n in range(NG_OUT)]
OUT_AT = [112, 116, 123]
OUT_T_AT = [111, 115, 122]


def hybrid_layer(nc, x, norm_mix, w_in, gla_a2, gla_ab, gla_norm, ml_conv, ml_ib, ml_fb, ml_norm,
                 sgu_ln_g, sgu_ln_b, sgu_w, sgu_b, w_out, norm_ffn, w_gu, w_down, norm_final, out):
    ctx = ExitStack()
    with ctx:
        def sb(name, shape, dt=F32, where=None):
            return (where or ctx).enter_context(nc.sbuf_tensor(name, shape, dt))

        sems = {}

        def sem(name):
            if name not in sems:
                sems[name] = ctx.enter_context(nc.semaphore(name))
            return sems[name]

        raw = sb("raw", [P, R, UC * GW])
        w_hi = sb("w_hi", [P, R, UC * GW], F32R)
        w_lo = sb("w_lo", [P, R, UC * GW], F32R)
        hT_hi = sb("hT_hi", [P, KC, T], F32R)
        hT_lo = sb("hT_lo", [P, KC, T], F32R)
        x1 = sb("x1", [P, NB, D])
        ident = sb("ident", [P, P])
        cols = sb("cols", [P, 36])
        stat = sb("stat", [P, 96])
        ss_x, ms_x, rs_x = stat[:, 0:2], stat[:, 2:4], stat[:, 4:6]
        ss_h, ms_h, rs_h = stat[:, 6:14], stat[:, 14:16], stat[:, 16:18]
        half_rs_h, half_rs2_h = stat[:, 18:20], stat[:, 20:22]
        ss_f, ms_f, rs_f = stat[:, 22:30], stat[:, 30:32], stat[:, 32:34]
        ss_a, ms_a, rs_a = stat[:, 34:42], stat[:, 42:50], stat[:, 50:58]
        minus_half = stat[:, 58:66]
        bn_c = stat[:, 66:78]
        mv_c = stat[:, 78:82]
        rs_c = stat[:, 82:84]
        tot_h, tot_f = stat[:, 84:86], stat[:, 86:88]
        stat_b = sb("stat_b", [P, 72])
        aT = stat_b[:, 0:8]
        mT = stat_b[:, 8:16]
        em = stat_b[:, 16:24]
        den = stat_b[:, 24:32]
        rden = stat_b[:, 32:40]
        ss_b, ms_b, rs_b, fac_b = stat_b[:, 40:48], stat_b[:, 48:56], stat_b[:, 56:64], stat_b[:, 64:72]

        early = ExitStack()
        tok = sb("tok", [P, NB, TOKW], where=early)
        mixT_hi = sb("mixT_hi", [P, KC, T], F32R, early)
        mixT_lo = sb("mixT_lo", [P, KC, T], F32R, early)
        qT = sb("qT", [DK, H, T], where=early)
        kT = sb("kT", [DK, H, T], where=early)
        cum = sb("cum", [DK, H, T], where=early)
        gwork = sb("gwork", [DK, 2080 + H * T], where=early)
        scA = sb("scA", [P, H, T], where=early)
        scB = sb("scB", [P, H, P], where=early)
        levels = sb("levels", [P, 8, P], I8, early)
        gates = sb("gates", [H, 6, T], where=early)
        cols96 = sb("cols96", [DK, 36], where=early)
        ib_fb = sb("ib_fb", [H, 2], where=early)
        a2 = sb("a2", [RANK, H * DK], where=early)
        ga1T = sb("ga1T", [RANK, T], where=early)
        ones = sb("ones", [P, T], where=early)
        early.close()
        late = ExitStack()
        actT_hi = sb("actT_hi", [P, FC, T], F32R, late)
        actT_lo = sb("actT_lo", [P, FC, T], F32R, late)
        gate_s = sb("gate_s", [P, NB, GW], where=late)
        act_tok = sb("act_tok", [P, NB, GW], where=late)
        nf_row = sb("nf_row", [P, D], where=late)
        late.close()

        xin = tok[:, :, :].rearrange("p b n -> p (b n)")[:, 0:NB * D].rearrange("p (b n) -> p b n", b=NB)
        junk = tok[:, :, :].rearrange("p b n -> p (b n)")[:, NB * D:NB * D + D]
        rowsA = tok[:, :, :].rearrange("p b n -> p (b n)")[0:36, 6200:6328]
        rowsB = tok[:, :, :].rearrange("p b n -> p (b n)")[0:36, 6400:6496]
        x1f = x1[:, :, :].rearrange("p b n -> p (b n)")
        gn_row, mn_row = x1f[:, 0:AW], x1f[:, AW:2 * AW]
        lng_row, lnb_row = x1f[:, 1536:2048], x1f[:, 2048:2560]
        sguw = x1f[:, 2560:3072].rearrange("p (g s) -> p g s", g=H)
        sguT = x1f[:, 3072:3584].rearrange("p (g s) -> p g s", g=H)
        sel = x1f[0:H, 3584:4096].rearrange("p (h n) -> p h n", h=H)
        g_dif = gwork[:, 0:H * T]
        g_q = gwork[:, H * T:2 * H * T]
        g_k = gwork[:, 2080:2080 + H * T]
        PAD = T + 4

        def gl_u(b):
            return tok[:, b, GG:GG + GW]

        def gl_v(b):
            return tok[:, b, GV:GV + GW]

        mraw = gwork[:, 0:2 * H * PAD].rearrange("p (g t) -> p g t", g=2 * H)
        cumf = cum[:, :, :].rearrange("p h t -> p (h t)")
        qTf = qT[:, :, :].rearrange("p h t -> p (h t)")
        kTf = kT[:, :, :].rearrange("p h t -> p (h t)")

        acc = ctx.enter_context(nc.psum_tensor("acc", [P, 4, GW], F32))
        mx = ctx.enter_context(nc.psum_tensor("mx", [P, 4, GW], F32))

        loaded = [sem(f"w_loaded{s}") for s in range(R)]
        hi_ready, lo_ready, unit_used = sem("w_hi_ready"), sem("w_lo_ready"), sem("unit_used")

        def weights(w, row0, c0, width):
            return w[row0:row0 + UC * P, bass.ds(c0, width)].rearrange("(k p) n -> p k n", p=P)

        block = ctx.enter_context(nc.Block())

        @block.sync
        def _(sp):
            def load(w, u, slot, row0, c0, width, first=False):
                if not first:
                    sp.wait_ge(lo_ready, u - R + 1)
                sp.dma_start(raw[:, slot, 0:UC * width].rearrange("p (k n) -> p k n", k=UC),
                             weights(w, row0, c0, width)).then_inc(loaded[slot], 16)

            for b in range(NB):
                for q in range(2):
                    sp.dma_start(xin[:, b, q * 1024:(q + 1) * 1024],
                                 x[b * P:(b + 1) * P, q * 1024:(q + 1) * 1024]).then_inc(sem(f"x_loaded{b}{q}"), 16)
            u = 0
            for c0, width, _at in IN_GROUPS:
                for k in range(UPG):
                    load(w_in, u, u % R, k * UC * P, c0, width, first=u < R)
                    u += 1
            for n, k in OUT_ORDER:
                load(w_out, u, u % R, k * UC * P, n * GW, GW)
                u += 1
            sp.wait_ge(unit_used, U_FF)
            sp.dma_start(nf_row[:, :], norm_final.partition_broadcast(P)).then_inc(sem("nf_loaded"), 16)
            with sp.Fori(0, NG_FF) as j:
                for k in range(2 * UPG):
                    load(w_gu, j * (2 * UPG) + (U_FF + k), k % R, (k % UPG) * UC * P,
                         j * GW + (FF if k >= UPG else 0), GW)
            with sp.Fori(0, NG_DN // 2) as i:
                for k in range(2 * UPD):
                    load(w_down, i * (2 * UPD) + (U_DN + k), k % R, (k % UPD) * UC * P,
                         i * (2 * GW) + (k // UPD) * GW, GW)
            for b in range(NB):
                for q in range(2):
                    sp.wait_ge(sem("y_ready"), b * 2 + q + 1)
                    sp.dma_start(out[b * P:(b + 1) * P, q * 1024:(q + 1) * 1024],
                                 x1[:, b, q * 1024:(q + 1) * 1024]).then_inc(sem("y_stored"), 16)
            sp.wait_ge(sem("y_stored"), 16 * 2 * NB)

        @block.gpsimd
        def _(pool):
            chain = [0]

            def link(ins):
                chain[0] += 1
                ins.then_inc(sem("pool_chain"), 1)
                pool.wait_ge(sem("pool_chain"), chain[0])

            link(pool.memset(ident[:, :], 0.0))
            pool.affine_select(out=ident[:, :], in_=ident[:, :], compare_op=ALU.not_equal, fill=1.0, base=0,
                               pattern=[[-1, P]], channel_multiplier=1).then_inc(sem("ident_ready"), 1)
            link(pool.memset(minus_half, -0.5))
            link(pool.memset(sel[:, :, :], 0.0))
            pool.affine_select(out=sel[:, :, :], in_=sel[:, :, :], compare_op=ALU.not_equal, fill=1.0, base=0,
                               pattern=[[-1, H], [0, P]], channel_multiplier=1).then_inc(sem("consts"), 1)
            pool.memset(ones[:, :], 1.0).then_inc(sem("consts"), 1)
            link(pool.memset(levels[:, :, :], 1.0))
            for i in range(7):
                half = 64 >> i
                v = levels[:, i, :].rearrange("p (b r) -> p b r", r=2 * half)
                nb = P // (2 * half)
                link(pool.affine_select(out=v, in_=v, compare_op=ALU.is_ge, fill=0.0, base=-half,
                                        pattern=[[0, nb], [1, 2 * half]], channel_multiplier=0))
                link(pool.affine_select(out=v, in_=v, compare_op=ALU.is_ge, fill=0.0, base=0,
                                        pattern=[[-2 * half, nb], [0, 2 * half]], channel_multiplier=1))
                link(pool.affine_select(out=v, in_=v, compare_op=ALU.is_ge, fill=0.0, base=half - 1,
                                        pattern=[[2 * half, nb], [0, 2 * half]], channel_multiplier=-1))
            pool.affine_select(out=levels[:, 7, :], in_=levels[:, 7, :], compare_op=ALU.is_equal, fill=0.0, base=0,
                               pattern=[[-1, P]], channel_multiplier=1).then_inc(sem("consts"), 1)
            pool.memset(scA[:, :, :], 0.0).then_inc(sem("consts"), 1)
            pool.memset(scB[:, :, :], 0.0).then_inc(sem("consts"), 1)
            pool.wait_ge(sem("sguw_loaded"), 16)
            pool.affine_select(out=sguw, in_=sguw, compare_op=ALU.is_ge, fill=0.0, base=0,
                               pattern=[[0, H], [-1, P]], channel_multiplier=1).then_inc(sem("sguw_tril"), 1)

            def rsqrt_mean(dst, tmp, total, n, eps, done):
                link(pool.tensor_scalar(tmp, total, 1.0 / n, eps, ALU.mult, ALU.add))
                pool.tensor_tensor(dst, tmp, minus_half[:, 0:dst.shape[1]], ALU.pow).then_inc(done, 1)

            pool.wait_ge(sem("x_squared"), NB)
            rsqrt_mean(rs_x, ms_x, ss_x, D, EPS, sem("rs_x_ready"))
            pool.wait_ge(sem("gla_squared"), NB * H)
            rsqrt_mean(rs_a, ms_a, ss_a, DV, EPS, sem("rs_a_ready"))
            pool.wait_ge(sem("bn_ready"), NB)
            rsqrt_mean(rs_c, mv_c.rearrange("p (b k) -> p b k", b=NB)[:, :, 1],
                       mv_c.rearrange("p (b k) -> p b k", b=NB)[:, :, 1], 1, 4 * EPS, sem("rs_c_ready"))
            pool.wait_ge(sem("ml_exp"), 2)
            pool.affine_select(out=scA[:, :, 0:P], in_=scA[:, :, 0:P], compare_op=ALU.is_ge, fill=0.0, base=0,
                               pattern=[[0, H], [1, P]], channel_multiplier=-1).then_inc(sem("ml_causal"), 1)
            pool.affine_select(out=scB[:, :, :], in_=scB[:, :, :], compare_op=ALU.is_ge, fill=0.0, base=0,
                               pattern=[[0, H], [1, P]], channel_multiplier=-1).then_inc(sem("ml_causal"), 1)
            pool.wait_ge(sem("ms_b_ready"), 1)
            rsqrt_mean(rs_b, ms_b, ms_b, 1, EPS, sem("rs_b_ready"))
            pool.wait_ge(sem("mix_lo"), MIXED_B)
            for b in range(NB):
                pool.dma_start(x1[:, b, :], x[b * P:(b + 1) * P, :]).then_inc(sem("x_again"), 16)
            pool.wait_ge(sem("tot_h_ready"), 1)
            rsqrt_mean(rs_h, ms_h, tot_h, D, EPS, sem("rs_h_ready"))
            pool.wait_ge(sem("tot_f_ready"), 1)
            rsqrt_mean(rs_f, ms_f, tot_f, D, EPS, sem("rs_f_ready"))

        @block.scalar
        def _(act):
            for dst, src in ((rowsA[0:KC, :], norm_mix.rearrange("(c p) -> c p", p=P)),
                             (rowsA[KC:2 * KC, :], norm_ffn.rearrange("(c p) -> c p", p=P)),
                             (rowsA[2 * KC:2 * KC + H, :], sgu_b),
                             (rowsB[0:H, :], gla_ab.rearrange("(h d) -> h d", d=DK)),
                             (rowsB[H:H + 32, :], ml_conv.rearrange("j (g d) -> (j g) d", d=DK))):
                act.dma_start(dst, src).then_inc(sem("rows_loaded"), 16)
            act.dma_start(sguw, sgu_w.rearrange("g t s -> t g s")).then_inc(sem("sguw_loaded"), 16)
            for dst, src in ((a2[:, :], gla_a2), (ib_fb[:, 0:1], ml_ib.rearrange("(h a) -> h a", a=1)),
                             (ib_fb[:, 1:2], ml_fb.rearrange("(h a) -> h a", a=1)),
                             (gn_row, gla_norm.partition_broadcast(P)), (mn_row, ml_norm.partition_broadcast(P)),
                             (lng_row, sgu_ln_g.partition_broadcast(P)), (lnb_row, sgu_ln_b.partition_broadcast(P))):
                act.dma_start(dst, src).then_inc(sem("small_loaded"), 16)

            def high(u, slot, width, uses, fresh=False):
                act.wait_ge(loaded[slot], uses)
                if not fresh:
                    act.wait_ge(unit_used, u - R + 1)
                act.activation(w_hi[:, slot, 0:UC * width], raw[:, slot, 0:UC * width], ACT.Copy)\
                   .then_inc(hi_ready, 1)

            def transposed_high(bank, c, dst, scale, done):
                for i in range(2):
                    act.activation(dst[:, c + i, :], mx[:, bank, i * T:(i + 1) * T], ACT.Copy, scale=scale(c + i))\
                       .then_inc(done, 1)

            def mix_high(batch, bank, c):
                act.wait_ge(sem("mixT_psum"), batch + 1)
                transposed_high(bank, c, mixT_hi, lambda _c: 0.5, sem("mix_hi"))

            def evacuate(g):
                _c0, width, at = IN_GROUPS[g]
                act.wait_ge(unit_used, (g + 1) * UPG)
                if g == 0:
                    act.wait_ge(sem("rs_x_ready"), 1)
                    act.wait_ge(sem("hT_lo_ready"), KC)
                if g == 8:
                    act.wait_ge(sem("gla_gate"), NB)
                if g == 9:
                    act.wait_ge(sem("ml_raw_psum"), 1)
                for b in range(NB):
                    act.activation(tok[:, b, at:at + width], acc[:, (g % 2) * 2 + b, 0:width], ACT.Copy,
                                   scale=rs_x[:, b:b + 1]).then_inc(sem("in_out"), 1)

            def softplus(buf, done):
                act.activation(buf, buf, ACT.Exp, scale=-1.0).then_inc(done, 1)
                act.wait_ge(done, 1)
                act.activation(buf, buf, ACT.Ln, bias=1.0).then_inc(done, 1)

            def squares(start, v0, ss, done):
                act.wait_ge(start, 1)
                for b in range(NB):
                    for h in range(H):
                        act.activation(tok[:, b, v0 + h * DV:v0 + (h + 1) * DV],
                                       mx[:, 2 * b + h // 2, (h % 2) * DV:(h % 2 + 1) * DV], ACT.Square,
                                       accum_out=ss[:, b * H + h:b * H + h + 1]).then_inc(done, 1)

            def out_squares(n):
                for b in range(NB):
                    act.wait_ge(sem("residual_added"), 2 * n + b + 1)
                    act.activation(scA[:, 0:2, :].rearrange("p h t -> p (h t)"), x1[:, b, n * GW:(n + 1) * GW],
                                   ACT.Square, accum_out=ss_h[:, b * NG_OUT + n:b * NG_OUT + n + 1])\
                       .then_inc(sem("h_squared"), 1)
                    act.wait_ge(sem("h_squared"), 2 * n + b + 1)

            def out_high(n):
                act.wait_ge(sem("x1T_psum"), n + 1)
                for i in range(2):
                    transposed_high((n % 2) * 2 + i, 4 * n + 2 * i, hT_hi, lambda c: cols[:, KC + c:KC + c + 1],
                                    sem("h2T_hi_ready"))

            act.wait_ge(sem("cols_ready"), 2)
            for b in range(KC // 2):
                act.wait_ge(sem("xT_psum"), b + 1)
                transposed_high(b % 4, 2 * b, hT_hi, lambda c: cols[:, c:c + 1], sem("hT_hi_ready"))
                if b % 2 == 1:
                    high(b // 2, b // 2, GW, 16, fresh=True)
            for b in range(NB):
                act.activation(junk, xin[:, b, :], ACT.Square, accum_out=ss_x[:, b:b + 1])\
                   .then_inc(sem("x_squared"), 1)
                act.wait_ge(sem("x_squared"), b + 1)
            act.wait_ge(sem("sguT_psum"), 1)
            act.activation(sguT, mx[:, 3, :].rearrange("p (g s) -> p g s", g=H), ACT.Copy).then_inc(sem("sguT_ready"), 1)

            for u in range(R, U_FF):
                g = u // UPG
                high(u, u % R, IN_GROUPS[g][1] if g < NG_IN else GW, 16 * (u // R + 1))
                if u % UPG == 3 and 1 <= g <= NG_IN:
                    evacuate(g - 1)
                if u == 23:
                    act.wait_ge(sem("gla_qk_psum"), 1)
                    act.activation(qTf, mx[0:DK, 0:2, :].rearrange("p k n -> p (k n)"), ACT.Copy,
                                   scale=DK ** -0.5).then_inc(sem("gla_qT"), 1)
                if u == 36:
                    act.wait_ge(sem("gla_abs"), 1)
                    softplus(g_dif, sem("gla_sp"))
                for i in range(8):
                    if u == LEVEL_AT + 4 * i:
                        act.wait_ge(sem("gla_dif"), 2 * (i + 1))
                        act.activation(g_dif, g_dif, ACT.Exp, scale=1.0 / TAU).then_inc(sem("gla_decay"), 1)
                if u == 45:
                    act.wait_ge(sem("in_out"), 2 * 5)
                    act.wait_ge(sem("gla_qk_psum"), 1)
                    for b in range(NB):
                        act.activation(tok[:, b, 0:AW], tok[:, b, GG:GG + AW], ACT.Tanh, scale=0.5)\
                           .then_inc(sem("gla_tanh"), 1)
                if u == AT_O_A + 4:
                    squares(sem("gla_o"), GV, ss_a, sem("gla_squared"))
                if u == AT_OT_A + 4:
                    for i in range(3):
                        mix_high(i, i, 2 * i)
                if u == AT_IF + 4:
                    act.wait_ge(sem("ml_abs"), 1)
                    softplus(gates[:, 3, :], sem("ml_sp"))
                if u == AT_RAW + 4:
                    act.wait_ge(sem("ml_raw_psum"), 1)
                    act.wait_ge(sem("ml_pad"), 1)
                    act.activation(mraw[:, 0:H, 3:3 + T], mx[0:DK, 0:2, :].rearrange("p k (h t) -> p (k h) t", t=T),
                                   ACT.Copy).then_inc(sem("ml_q_raw"), 1)
                if u == AT_MB + 4:
                    act.wait_ge(sem("ml_dif"), 2 * H + 1)
                    act.activation(scA[:, :, :], scA[:, :, :], ACT.Exp, scale=-1.0).then_inc(sem("ml_exp"), 1)
                    act.activation(scB[:, :, :], scB[:, :, :], ACT.Exp, scale=-1.0).then_inc(sem("ml_exp"), 1)
                    act.activation(em, mT, ACT.Exp, scale=-1.0).then_inc(sem("ml_em"), 1)
                if u == AT_CONV + 8:
                    act.wait_ge(sem("ml_conv_done"), 8)
                    act.activation(gwork[:, 0:H * T], qTf, ACT.Tanh, scale=0.5).then_inc(sem("ml_tanh"), 1)
                    act.activation(gwork[:, H * T:2 * H * T], kTf, ACT.Tanh, scale=0.5).then_inc(sem("ml_tanh"), 1)
                if u == AT_GELU:
                    act.wait_ge(sem("in_out"), 2 * 10)
                    act.wait_ge(sem("mixT_psum"), 3)
                    act.wait_ge(sem("gla_out"), NB * H)
                    for b in range(NB):
                        act.activation(gl_u(b), tok[:, b, MQ:MQ + GW], ACT.Square).then_inc(sem("gelu_sq"), 1)
                        act.activation(gl_v(b), tok[:, b, 0:GW], ACT.Square).then_inc(sem("gelu_sq"), 1)
                if u == AT_GELU + 2:
                    for b in range(NB):
                        act.wait_ge(sem("gelu_arg"), 2 * b + 2)
                        act.activation(gl_u(b), gl_u(b), ACT.Tanh, scale=GELU_C0).then_inc(sem("gelu_tanh"), 1)
                        act.activation(gl_v(b), gl_v(b), ACT.Tanh, scale=GELU_C0).then_inc(sem("gelu_tanh"), 1)
                if u == AT_OT_C + 4:
                    mix_high(3, 0, 12)
                    mix_high(4, 1, 14)
                if u == AT_MO:
                    act.wait_ge(sem("in_out"), 2 * NG_IN)
                    act.wait_ge(sem("mixT_psum"), 5)
                    for b in range(NB):
                        act.activation(tok[:, b, MQ:MQ + AW], tok[:, b, MO:MO + AW], ACT.Tanh, scale=0.5)\
                           .then_inc(sem("ml_gate_tanh"), 1)
                if u == AT_O_B + 4:
                    squares(sem("ml_o"), MV, ss_b, sem("ml_squared"))
                if u == AT_OT_B + 4:
                    for i in range(3):
                        mix_high(5 + i, i, 6 + 2 * i)
                for n in range(NG_OUT - 1):
                    if u == OUT_AT[n]:
                        out_squares(n)
                    if u == OUT_T_AT[n] + 4:
                        out_high(n)
            out_squares(NG_OUT - 1)
            out_high(NG_OUT - 1)

            def gate_tanh(used, gates_read=None):
                act.wait_ge(unit_used, used)
                if gates_read is not None:
                    act.wait_ge(sem("act_ready"), gates_read)
                for b in range(NB):
                    act.activation(gate_s[:, b, :], acc[:, b, :], ACT.Tanh, scale=half_rs_h[:, b:b + 1])\
                       .then_inc(sem("gate_tanh"), 1)

            def act_high(groups, c):
                act.wait_ge(sem("actT_psum"), groups)
                act.activation(actT_hi[:, bass.ds(c, 4), :].rearrange("p c t -> p (c t)"),
                               mx[:, 0:2, :].rearrange("p k n -> p (k n)"), ACT.Copy).then_inc(sem("act_hi"), 1)

            def gate_up(j, peeled):
                for k in range(2 * UPG):
                    high(j * (2 * UPG) + (U_FF + k), k % R, GW, j * (16 * 2 * UPG // R) + 16 * ((U_FF + k) // R + 1))
                    if k == 9 and not peeled:
                        act_high(j, j * 4 - 4)
                    if k == 11:
                        if peeled:
                            act.wait_ge(sem("rs_h2_ready"), 1)
                        gate_tanh(j * (2 * UPG) + (U_FF + UPG), None if peeled else j * 2)

            gate_up(0, True)
            with act.Fori(1, NG_FF) as j:
                gate_up(j, False)
            act_high(NG_FF, 4 * (NG_FF - 1))

            with act.Fori(0, NG_DN // 2) as i:
                for k in range(2 * UPD):
                    high(i * (2 * UPD) + (U_DN + k), k % R, GW, i * (16 * 2 * UPD // R) + 16 * ((U_DN + k) // R + 1))
            f_junk = gate_s[:, :, :].rearrange("p b n -> p (b n)")
            act.wait_ge(sem("residual_added"), 2 * NG_OUT + 2 * NG_DN)
            for b in range(NB):
                for q in range(2):
                    act.activation(f_junk, x1[:, b, q * 1024:(q + 1) * 1024], ACT.Square,
                                   accum_out=ss_f[:, 2 * b + q:2 * b + q + 1]).then_inc(sem("f_squared"), 1)
                    act.wait_ge(sem("f_squared"), 2 * b + q + 1)

        @block.vector
        def _(dve):
            chain = [0]

            def step(ins):
                chain[0] += 1
                ins.then_inc(sem("dve_chain"), 1)

            def settle():
                dve.wait_ge(sem("dve_chain"), chain[0])

            def low(u, slot, width):
                dve.wait_ge(hi_ready, u + 1)
                dve.tensor_tensor(w_lo[:, slot, 0:UC * width], raw[:, slot, 0:UC * width],
                                  w_hi[:, slot, 0:UC * width].bitcast(F32), ALU.subtract).then_inc(lo_ready, 1)

            def transposed_low(bank, c, hi, lo, scale, done):
                for i in range(2):
                    dve.scalar_tensor_tensor(out=lo[:, c + i, :], in0=mx[:, bank, i * T:(i + 1) * T], scalar=scale(c + i),
                                             in1=hi[:, c + i, :].bitcast(F32), op0=ALU.mult, op1=ALU.subtract)\
                       .then_inc(done, 1)

            def mix_low(batch, bank, c):
                dve.wait_ge(sem("mix_hi"), 2 * (batch + 1))
                transposed_low(bank, c, mixT_hi, mixT_lo, lambda _c: 0.5, sem("mix_lo"))

            dve.wait_ge(sem("colsT_psum"), 1)
            dve.tensor_copy(cols[:, :], mx[:, 0, 0:36]).then_inc(sem("cols_ready"), 1)
            dve.tensor_copy(cols96[:, :], mx[0:DK, 1, 0:36]).then_inc(sem("cols_ready"), 1)
            for b in range(KC // 2):
                dve.wait_ge(sem("hT_hi_ready"), 2 * (b + 1))
                transposed_low(b % 4, 2 * b, hT_hi, hT_lo, lambda c: cols[:, c:c + 1], sem("hT_lo_ready"))
                if b % 2 == 1:
                    low(b // 2, b // 2, GW)

            def gla_logsig():
                dve.wait_ge(sem("gla_pre_psum"), 1)
                for h in range(H):
                    step(dve.tensor_scalar(cum[:, h, :], mx[0:DK, 2 + h // 2, (h % 2) * T:(h % 2 + 1) * T],
                                           cols96[:, h:h + 1], None, ALU.add))
                settle()
                step(dve.tensor_scalar(g_q, cumf, 0.0, None, ALU.min))
                settle()
                dve.scalar_tensor_tensor(out=g_dif, in0=g_q, scalar=-2.0, in1=cumf, op0=ALU.mult, op1=ALU.add)\
                   .then_inc(sem("gla_abs"), 1)

            def gla_cumulate():
                dve.wait_ge(sem("gla_sp"), 2)
                dve.wait_ge(sem("consts"), 5)
                step(dve.tensor_tensor(g_q, g_q, g_dif, ALU.subtract))
                settle()
                for h in range(H):
                    step(dve.tensor_tensor_scan(cum[:, h, :], ones[0:DK, :], g_q[:, h * T:(h + 1) * T], 0.0,
                                                ALU.mult, ALU.add))
                settle()

            def gla_differences(i):
                half = P >> i
                if i == 0:
                    c = cumf.rearrange("p (n a r) -> p n a r", a=2, r=half)
                    d = g_dif.rearrange("p (n a r) -> p n a r", a=2, r=half)
                else:
                    dve.wait_ge(sem("gla_prod"), 2 * i)
                    c = cumf.rearrange("p (n a r) -> p n a r", a=2, r=half)
                    d = g_dif.rearrange("p (n a r) -> p n a r", a=2, r=half)
                n = H * T // (2 * half)
                ref = c[:, :, 0, half - 1:half].to_broadcast([DK, n, half])
                dve.tensor_tensor(d[:, :, 0, :], ref, c[:, :, 0, :], ALU.subtract).then_inc(sem("gla_dif"), 1)
                dve.tensor_tensor(d[:, :, 1, :], c[:, :, 1, :], ref, ALU.subtract).then_inc(sem("gla_dif"), 1)

            def gla_products(i):
                dve.wait_ge(sem("gla_decay"), i + 1)
                if i > 0:
                    dve.wait_ge(sem("gla_lev_psum"), i + 1)
                dve.tensor_tensor(g_q, qTf, g_dif, ALU.mult).then_inc(sem("gla_prod"), 1)
                dve.tensor_tensor(g_k, kTf, g_dif, ALU.mult).then_inc(sem("gla_prod"), 1)

            def gla_pick(i, bank):
                for b, dst in enumerate((scA[:, :, 0:P], scB[:, :, :])):
                    dve.copy_predicated(dst, levels[:, i, :].unsqueeze(1).to_broadcast([P, H, P]),
                                        mx[:, bank + b, :].rearrange("p (h t) -> p h t", h=H))\
                       .then_inc(sem("gla_pick"), 1)

            def out_add(n):
                dve.wait_ge(unit_used, OUT_DONE[n])
                dve.wait_ge(sem("x_again"), 16 * NB)
                for b in range(NB):
                    dst = x1[:, b, n * GW:(n + 1) * GW]
                    dve.tensor_tensor(dst, acc[:, 2 * (n % 2) + b, :], dst, ALU.add).then_inc(sem("residual_added"), 1)

            def out_low(n):
                for i in range(2):
                    dve.wait_ge(sem("h2T_hi_ready"), 4 * n + 2 * i + 2)
                    transposed_low((n % 2) * 2 + i, 4 * n + 2 * i, hT_hi, hT_lo, lambda c: cols[:, KC + c:KC + c + 1],
                                   sem("h2T_lo_ready"))

            for u in range(R, U_FF):
                g = u // UPG
                low(u, u % R, IN_GROUPS[g][1] if g < NG_IN else GW)
                if u == 23:
                    dve.wait_ge(sem("gla_qk_psum"), 1)
                    dve.tensor_copy(kTf, mx[0:DK, 2:4, :].rearrange("p k n -> p (k n)")).then_inc(sem("gla_kT"), 1)
                if u == 28:
                    dve.wait_ge(sem("gla_lev_psum"), 1)
                    dve.wait_ge(sem("consts"), 5)
                    gla_pick(7, 0)
                if u == 31:
                    dve.wait_ge(sem("ga1T_psum"), 1)
                    dve.tensor_copy(ga1T[:, :], mx[0:RANK, 2, 0:T]).then_inc(sem("ga1T_ready"), 1)
                if u == 35:
                    gla_logsig()
                if u == 37:
                    gla_cumulate()
                for i in range(8):
                    if u == LEVEL_AT + 4 * i:
                        gla_differences(i)
                    if u == LEVEL_AT + 4 * i + 1:
                        gla_products(i)
                    if u == LEVEL_AT + 4 * i + 5:
                        dve.wait_ge(sem("gla_lev_psum"), i + 2)
                        if i == 0:
                            dve.tensor_copy(scA[:, :, P:T], mx[:, 0, :].rearrange("p (h t) -> p h t", h=H))\
                               .then_inc(sem("gla_pick"), 1)
                        else:
                            gla_pick(i - 1, 2 * (i % 2))
                if u in (46, 50):
                    b = (u - 46) // 4
                    dve.wait_ge(sem("gla_tanh"), b + 1)
                    dve.wait_ge(sem("small_loaded"), 16 * 7)
                    step(dve.scalar_tensor_tensor(out=tok[:, b, GG:GG + AW], in0=tok[:, b, 0:AW], scalar=1.0,
                                                  in1=tok[:, b, GG:GG + AW], op0=ALU.add, op1=ALU.mult))
                    settle()
                    dve.tensor_tensor(tok[:, b, GG:GG + AW], tok[:, b, GG:GG + AW], gn_row, ALU.mult)\
                       .then_inc(sem("gla_gate"), 1)
                if u == AT_O_A + 5:
                    dve.wait_ge(sem("rs_a_ready"), 1)
                    dve.wait_ge(sem("gla_gate"), NB)
                    for b in range(NB):
                        for h in range(H):
                            dst = tok[:, b, GG + h * DV:GG + (h + 1) * DV]
                            dve.scalar_tensor_tensor(out=dst, in0=mx[:, 2 * b + h // 2, (h % 2) * DV:(h % 2 + 1) * DV],
                                                     scalar=rs_a[:, b * H + h:b * H + h + 1], in1=dst,
                                                     op0=ALU.mult, op1=ALU.mult).then_inc(sem("gla_out"), 1)
                if u == AT_OT_A + 4:
                    for i in range(3):
                        mix_low(i, i, 2 * i)
                if u == AT_IF + 4:
                    dve.wait_ge(sem("ml_if_psum"), 1)
                    step(dve.tensor_scalar(gates[:, 0, :], mx[0:H, 3, 0:T], ib_fb[:, 0:1], None, ALU.add))
                    step(dve.tensor_scalar(gates[:, 1, :], mx[0:H, 3, T:2 * T], ib_fb[:, 1:2], None, ALU.add))
                    settle()
                    step(dve.tensor_scalar(gates[:, 2, :], gates[:, 1, :], 0.0, None, ALU.min))
                    settle()
                    dve.scalar_tensor_tensor(out=gates[:, 3, :], in0=gates[:, 2, :], scalar=-2.0, in1=gates[:, 1, :],
                                             op0=ALU.mult, op1=ALU.add).then_inc(sem("ml_abs"), 1)
                if u == AT_IF + 5:
                    dve.wait_ge(sem("ml_sp"), 2)
                    step(dve.tensor_tensor(gates[:, 2, :], gates[:, 2, :], gates[:, 3, :], ALU.subtract))
                    settle()
                    step(dve.tensor_tensor_scan(gates[:, 4, :], ones[0:H, :], gates[:, 2, :], 0.0, ALU.mult, ALU.add))
                    settle()
                    step(dve.tensor_tensor(gates[:, 5, :], gates[:, 0, :], gates[:, 4, :], ALU.subtract))
                    settle()
                    step(dve.tensor_tensor_scan(gates[:, 3, :], gates[:, 5, :], gates[:, 5, :], 0.0, ALU.max, ALU.max))
                    settle()
                    dve.tensor_tensor(gates[:, 1, :], gates[:, 4, :], gates[:, 3, :], ALU.add).then_inc(sem("ml_m"), 1)
                if u == AT_RAW + 3:
                    dve.wait_ge(sem("gla_lev_psum"), 9)
                    dve.memset(mraw[:, :, 0:3], 0.0).then_inc(sem("ml_pad"), 1)
                if u == AT_RAW + 4:
                    dve.wait_ge(sem("ml_raw_psum"), 1)
                    dve.tensor_copy(mraw[:, H:2 * H, 3:3 + T], mx[0:DK, 2:4, :].rearrange("p k (h t) -> p (k h) t", t=T))\
                       .then_inc(sem("ml_k_raw"), 1)
                for c in range(2 * H):
                    if u == AT_CONV + c:
                        dve.wait_ge(sem("ml_q_raw"), 1)
                        dve.wait_ge(sem("ml_k_raw"), 1)
                        dst = (qT if c < H else kT)[:, c % H, :]
                        step(dve.tensor_scalar(dst, mraw[:, c, 0:T], cols96[:, H + c:H + c + 1], None, ALU.mult))
                        for tap in range(1, 4):
                            settle()
                            w = cols96[:, H + 8 * tap + c:H + 8 * tap + c + 1]
                            ins = dve.scalar_tensor_tensor(out=dst, in0=mraw[:, c, tap:tap + T], scalar=w, in1=dst,
                                                           op0=ALU.mult, op1=ALU.add)
                            if tap < 3:
                                step(ins)
                            else:
                                ins.then_inc(sem("ml_conv_done"), 1)
                if u == AT_CONV + 9:
                    for i, t in enumerate((qTf, kTf)):
                        dve.wait_ge(sem("ml_tanh"), i + 1)
                        dve.scalar_tensor_tensor(out=t, in0=gwork[:, i * H * T:(i + 1) * H * T], scalar=1.0, in1=t,
                                                 op0=ALU.add, op1=ALU.mult).then_inc(sem("ml_qk"), 1)
                if u == AT_MB + 4:
                    dve.wait_ge(sem("ml_mb_psum"), 1)
                    dve.tensor_copy(stat_b[:, 0:16], mx[:, 0, 0:16]).then_inc(sem("ml_dif"), 1)
                    dve.wait_ge(sem("ml_dif"), 1)
                    for h in range(H):
                        mb = mx[:, 2 + h // 2, (h % 2) * T:(h % 2 + 1) * T]
                        dve.tensor_scalar(scA[:, h, :], mb, aT[:, h:h + 1], 0.0, ALU.subtract, ALU.max)\
                           .then_inc(sem("ml_dif"), 1)
                        dve.tensor_scalar(scB[:, h, :], mb[:, P:T], aT[:, H + h:H + h + 1], 0.0, ALU.subtract, ALU.max)\
                           .then_inc(sem("ml_dif"), 1)
                if u == AT_GELU + 1:
                    for b in range(NB):
                        for k, (buf, src) in enumerate(((gl_u(b), tok[:, b, MQ:MQ + GW]), (gl_v(b), tok[:, b, 0:GW]))):
                            dve.wait_ge(sem("gelu_sq"), 2 * b + k + 1)
                            step(dve.tensor_scalar(buf, buf, GELU_C1, 1.0, ALU.mult, ALU.add))
                            settle()
                            dve.tensor_tensor(buf, buf, src, ALU.mult).then_inc(sem("gelu_arg"), 1)
                if u == AT_GELU + 3:
                    for b in range(NB):
                        for k, (buf, src) in enumerate(((gl_u(b), tok[:, b, MQ:MQ + GW]), (gl_v(b), tok[:, b, 0:GW]))):
                            dve.wait_ge(sem("gelu_tanh"), 2 * b + k + 1)
                            step(dve.scalar_tensor_tensor(out=src, in0=buf, scalar=1.0, in1=src,
                                                          op0=ALU.add, op1=ALU.mult))
                        settle()
                        step(dve.bn_stats(out=bn_c[:, 6 * b:6 * b + 6], in_=tok[:, b, 0:GW]))
                        settle()
                        dve.bn_aggr(out=mv_c[:, 2 * b:2 * b + 2], in_=bn_c[:, 6 * b:6 * b + 6])\
                           .then_inc(sem("bn_ready"), 1)
                if u == AT_GELU + 5:
                    dve.wait_ge(sem("rs_c_ready"), 1)
                    for b in range(NB):
                        v = tok[:, b, 0:GW]
                        step(dve.tensor_scalar(v, v, mv_c[:, 2 * b:2 * b + 1], rs_c[:, b:b + 1], ALU.subtract, ALU.mult))
                        settle()
                        step(dve.tensor_tensor(v, v, lng_row, ALU.mult))
                        settle()
                        dve.tensor_tensor(v, v, lnb_row, ALU.add).then_inc(sem("sgu_v"), 1)
                if u == AT_MIXED + 4:
                    dve.wait_ge(sem("sgu_psum"), 1)
                    for b in range(NB):
                        for h in range(H):
                            dst = tok[:, b, MQ + h * P:MQ + (h + 1) * P]
                            dve.scalar_tensor_tensor(out=dst, in0=mx[:, b, h * P:(h + 1) * P],
                                                     scalar=cols[:, 2 * KC + h:2 * KC + h + 1], in1=dst,
                                                     op0=ALU.add, op1=ALU.mult).then_inc(sem("sgu_out"), 1)
                if u == AT_OT_C + 4:
                    mix_low(3, 0, 12)
                    mix_low(4, 1, 14)
                if u == AT_SC + 3:
                    dve.wait_ge(sem("ml_sc_psum"), 1)
                    dve.wait_ge(sem("ml_causal"), 2)
                    scale = 0.25 * DK ** -0.5
                    for s, src in ((scA[:, :, :], mx[:, 2:4, :].rearrange("p k n -> p (k n)")), (scB[:, :, :], mx[:, 1, :])):
                        s = s.rearrange("p h t -> p (h t)")
                        dve.scalar_tensor_tensor(out=s, in0=src, scalar=scale, in1=s, op0=ALU.mult, op1=ALU.mult)\
                           .then_inc(sem("ml_scored"), 1)
                if u == AT_MO + 2:
                    for b in range(NB):
                        dve.wait_ge(sem("ml_gate_tanh"), b + 1)
                        dve.scalar_tensor_tensor(out=tok[:, b, MO:MO + AW], in0=tok[:, b, MQ:MQ + AW], scalar=1.0,
                                                 in1=mn_row, op0=ALU.add, op1=ALU.mult).then_inc(sem("ml_gate"), 1)
                if u == AT_O_B + 4:
                    dve.wait_ge(sem("ml_squared"), NB * H)
                    dve.wait_ge(sem("ml_em"), 1)
                    dview = den.rearrange("p (k h) -> p k h", h=2)
                    step(dve.tensor_copy(dview, mx[:, :, 2 * DV:2 * DV + 2]))
                    settle()
                    step(dve.scalar_tensor_tensor(out=rden, in0=den, scalar=-1.0, in1=den, op0=ALU.mult, op1=ALU.max))
                    settle()
                    step(dve.tensor_tensor(rden, rden, em, ALU.max))
                    settle()
                    step(dve.reciprocal(rden, rden))
                    settle()
                    step(dve.tensor_tensor(ms_b, ss_b, rden, ALU.mult))
                    settle()
                    step(dve.tensor_tensor(ms_b, ms_b, rden, ALU.mult))
                    settle()
                    dve.tensor_scalar(ms_b, ms_b, 1.0 / DV, None, ALU.mult).then_inc(sem("ms_b_ready"), 1)
                    dve.wait_ge(sem("rs_b_ready"), 1)
                    step(dve.tensor_tensor(fac_b, rden, rs_b, ALU.mult))
                    settle()
                    dve.wait_ge(sem("ml_gate"), NB)
                    for b in range(NB):
                        for h in range(H):
                            dst = tok[:, b, MO + h * DV:MO + (h + 1) * DV]
                            dve.scalar_tensor_tensor(out=dst, in0=mx[:, 2 * b + h // 2, (h % 2) * DV:(h % 2 + 1) * DV],
                                                     scalar=fac_b[:, b * H + h:b * H + h + 1], in1=dst,
                                                     op0=ALU.mult, op1=ALU.mult).then_inc(sem("ml_out"), 1)
                if u == AT_OT_B + 4:
                    for i in range(3):
                        mix_low(5 + i, i, 6 + 2 * i)
                for n in range(NG_OUT - 1):
                    if u == OUT_AT[n]:
                        out_add(n)
                    if u == OUT_T_AT[n] + 4:
                        out_low(n)
            out_add(NG_OUT - 1)
            out_low(NG_OUT - 1)
            dve.wait_ge(sem("h_squared"), 2 * NG_OUT)
            dve.tensor_reduce(out=tot_h, in_=ss_h.rearrange("p (b n) -> p b n", b=NB), axis=AX_X, op=ALU.add)\
               .then_inc(sem("tot_h_ready"), 1)

            def gated(tanhs):
                for b in range(NB):
                    dve.wait_ge(sem("gate_tanh"), tanhs + b + 1)
                    dve.scalar_tensor_tensor(out=gate_s[:, b, :], in0=gate_s[:, b, :], scalar=1.0, in1=acc[:, b, :],
                                             op0=ALU.add, op1=ALU.mult).then_inc(sem("gate_used"), 1)

            def activate(used, gates_done, transposed=None):
                dve.wait_ge(unit_used, used)
                dve.wait_ge(sem("gate_used"), gates_done)
                if transposed is not None:
                    dve.wait_ge(sem("actT_psum"), transposed)
                for b in range(NB):
                    dve.scalar_tensor_tensor(out=act_tok[:, b, :], in0=acc[:, 2 + b, :], scalar=half_rs2_h[:, b:b + 1],
                                             in1=gate_s[:, b, :], op0=ALU.mult, op1=ALU.mult)\
                       .then_inc(sem("act_ready"), 1)

            def act_low(groups, c):
                dve.wait_ge(sem("act_hi"), groups)
                d = bass.ds(c, 4)
                dve.tensor_tensor(actT_lo[:, d, :].rearrange("p c t -> p (c t)"), mx[:, 0:2, :].rearrange("p k n -> p (k n)"),
                                  actT_hi[:, d, :].rearrange("p c t -> p (c t)").bitcast(F32), ALU.subtract)\
                   .then_inc(sem("act_lo"), 1)

            def gate_up(j, peeled, after_first=False):
                for k in range(2 * UPG):
                    low(j * (2 * UPG) + (U_FF + k), k % R, GW)
                    if k == 3 and not peeled:
                        activate(j * (2 * UPG) + U_FF, j * 2, None if after_first else j - 1)
                    if k == 9 and not peeled:
                        act_low(j, j * 4 - 4)
                    if k == 11:
                        if peeled:
                            dve.wait_ge(sem("rs_h_ready"), 1)
                            step(dve.tensor_tensor(half_rs2_h, rs_h, rs_h, ALU.mult))
                            dve.tensor_scalar(half_rs_h, rs_h, 0.5, None, ALU.mult).then_inc(sem("rs_h2_ready"), 1)
                            settle()
                            step(dve.tensor_scalar(half_rs2_h, half_rs2_h, 0.5, None, ALU.mult))
                            settle()
                        gated(j * 2)

            gate_up(0, True)
            gate_up(1, False, True)
            with dve.Fori(2, NG_FF) as j:
                gate_up(j, False)
            activate(U_DN, 2 * NG_FF, NG_FF - 1)
            act_low(NG_FF, 4 * (NG_FF - 1))

            def down_add(n, m, used):
                dve.wait_ge(unit_used, used)
                for b in range(NB):
                    dst = x1[:, b, bass.ds(n * GW, GW)]
                    dve.tensor_tensor(dst, acc[:, 2 * m + b, :], dst, ALU.add).then_inc(sem("residual_added"), 1)

            with dve.Fori(0, NG_DN // 2) as i:
                for k in range(2 * UPD):
                    low(i * (2 * UPD) + (U_DN + k), k % R, GW)
                    if k == UPD + 3:
                        down_add(i * 2, 0, i * (2 * UPD) + (U_DN + UPD))
                down_add(i * 2 + 1, 1, i * (2 * UPD) + (U_DN + 2 * UPD))
            dve.wait_ge(sem("f_squared"), 2 * NB)
            dve.tensor_reduce(out=tot_f, in_=ss_f[:, 0:4].rearrange("p (b q) -> p b q", b=NB), axis=AX_X, op=ALU.add)\
               .then_inc(sem("tot_f_ready"), 1)
            dve.wait_ge(sem("rs_f_ready"), 1)
            dve.wait_ge(sem("nf_loaded"), 16)
            for b in range(NB):
                for q in range(2):
                    y = x1[:, b, q * 1024:(q + 1) * 1024]
                    dve.scalar_tensor_tensor(out=y, in0=y, scalar=rs_f[:, b:b + 1], in1=nf_row[:, q * 1024:(q + 1) * 1024],
                                             op0=ALU.mult, op1=ALU.mult).then_inc(sem("y_ready"), 1)

        @block.tensor
        def _(pe):
            def transpose(dst, src, n):
                return pe.transpose(dst, src, ident[0:n, 0:n])

            def unit(u, slot, width, hi, lo, c, bank, first, last):
                pe.wait_ge(lo_ready, u + 1)
                for i in range(UC):
                    for b in range(NB):
                        o = acc[:, bank + b, 0:width]
                        tb = slice(b * P, (b + 1) * P)
                        wh, wl = (w[:, slot, i * width:(i + 1) * width] for w in (w_hi, w_lo))
                        pe.matmul(o, hi[:, c + i, tb], wh, start=first and i == 0, stop=False)
                        pe.matmul(o, hi[:, c + i, tb], wl, start=False, stop=False)
                        ins = pe.matmul(o, lo[:, c + i, tb], wh, start=False, stop=last and i == UC - 1)
                ins.then_inc(unit_used, 1)

            pe.wait_ge(sem("ident_ready"), 1)
            pe.wait_ge(sem("rows_loaded"), 16 * 5)
            transpose(mx[:, 0, 0:36], rowsA, 36)
            transpose(mx[0:DK, 1, 0:36], rowsB, 36).then_inc(sem("colsT_psum"), 1)
            for b in range(KC // 2):
                if b < 4:
                    if b < 2:
                        pe.wait_ge(sem("cols_ready"), 2)
                else:
                    pe.wait_ge(sem("hT_lo_ready"), 2 * (b - 3))
                for i in range(2):
                    for t in range(NB):
                        if i == 0 and b % 4 == 0:
                            pe.wait_ge(sem(f"x_loaded{t}{b // 4}"), 16)
                        c = 2 * b + i
                        ins = transpose(mx[:, b % 4, i * T + t * P:i * T + (t + 1) * P], xin[:, t, c * P:(c + 1) * P], P)
                ins.then_inc(sem("xT_psum"), 1)
            pe.wait_ge(sem("sguw_tril"), 1)
            pe.wait_ge(sem("hT_lo_ready"), KC)
            for g in range(H):
                ins = transpose(mx[:, 3, g * P:(g + 1) * P], sguw[:, g, :], P)
            ins.then_inc(sem("sguT_psum"), 1)

            def heads_transposed(q0, k0, done):
                for s, c0 in enumerate((q0, k0)):
                    for h in range(H):
                        for b in range(NB):
                            ins = transpose(mx[0:DK, 2 * s + h // 2, (h % 2) * T + b * P:(h % 2) * T + (b + 1) * P],
                                            tok[:, b, c0 + h * DK:c0 + (h + 1) * DK], P)
                ins.then_inc(done, 1)

            def scores(q, k, bank):
                for b in range(NB):
                    for h in range(H):
                        at = slice(h * T + b * P, h * T + (b + 1) * P)
                        ins = pe.matmul(mx[:, bank + b, h * P:(h + 1) * P], k[:, at], q[:, at], start=True, stop=True)
                return ins

            def attend(v0, with_den):
                for b in range(NB):
                    for h in range(H):
                        bank = 2 * b + h // 2
                        for lo, width, is_den in (((h % 2) * DV, DV, False), (2 * DV + h % 2, 1, True)):
                            if is_den and not with_den:
                                continue
                            o = mx[:, bank, lo:lo + width]
                            terms = [(scA[:, h, b * P:(b + 1) * P], 0)] + ([(scB[:, h, :], 1)] if b else [])
                            for n, (s, kb) in enumerate(terms):
                                v = ones[:, 0:1] if is_den else tok[:, kb, v0 + h * DV:v0 + (h + 1) * DV]
                                ins = pe.matmul(o, s, v, start=n == 0, stop=n == len(terms) - 1)
                return ins

            def mixed_transposed(banks, columns):
                for bank, c0 in zip(banks, columns):
                    for i in range(2):
                        for b in range(NB):
                            ins = transpose(mx[:, bank, i * T + b * P:i * T + (b + 1) * P],
                                            tok[:, b, c0 + i * P:c0 + (i + 1) * P], P)
                    ins.then_inc(sem("mixT_psum"), 1)

            def x1_transposed(n):
                pe.wait_ge(sem("residual_added"), 2 * (n + 1))
                if n < 2:
                    pe.wait_ge(sem("mix_lo"), MIXED_B)
                else:
                    pe.wait_ge(sem("h2T_lo_ready"), 4 * (n - 1))
                for i in range(4):
                    for b in range(NB):
                        c = 4 * n + i
                        ins = transpose(mx[:, (n % 2) * 2 + i // 2, (i % 2) * T + b * P:(i % 2) * T + (b + 1) * P],
                                        x1[:, b, c * P:(c + 1) * P], P)
                ins.then_inc(sem("x1T_psum"), 1)

            for u in range(U_FF):
                g, k = divmod(u, UPG)
                if g < NG_IN:
                    if g == 0:
                        pe.wait_ge(sem("hT_lo_ready"), UC * (k + 1))
                    if g >= 2 and k == 0:
                        pe.wait_ge(sem("in_out"), 2 * (g - 1))
                    unit(u, u % R, IN_GROUPS[g][1], hT_hi, hT_lo, UC * k, 2 * (g % 2), k == 0, k == UPG - 1)
                else:
                    i = u - U_OUT
                    n, k = OUT_ORDER[i]
                    done = [q for m, q in OUT_ORDER[:i] if m == n]
                    if not done:
                        if n < 2:
                            pe.wait_ge(sem("in_out"), 2 * (NG_IN - 1 + n))
                        else:
                            pe.wait_ge(sem("residual_added"), 2 * (n - 1))
                    pe.wait_ge(sem("mix_lo"), MIXED_A if k in MIX_A else MIXED_C if k in MIX_C else MIXED_B)
                    unit(u, u % R, GW, mixT_hi, mixT_lo, UC * k, 2 * (n % 2), not done, len(done) == UPG - 1)
                if u == 19:
                    pe.wait_ge(sem("in_out"), 4)
                    pe.wait_ge(sem("sguT_ready"), 1)
                    heads_transposed(GQ, GK, sem("gla_qk_psum"))
                if u == 24:
                    pe.wait_ge(sem("gla_qT"), 1)
                    pe.wait_ge(sem("gla_kT"), 1)
                    scores(qTf, kTf, 0).then_inc(sem("gla_lev_psum"), 1)
                if u == 27:
                    pe.wait_ge(sem("in_out"), 6)
                    for b in range(NB):
                        ins = transpose(mx[0:RANK, 2, b * P:(b + 1) * P], tok[:, b, GA1:GA1 + RANK], P)
                    ins.then_inc(sem("ga1T_psum"), 1)
                if u == 31:
                    pe.wait_ge(sem("ga1T_ready"), 1)
                    pe.wait_ge(sem("small_loaded"), 16 * 7)
                    for h in range(H):
                        ins = pe.matmul(mx[0:DK, 2 + h // 2, (h % 2) * T:(h % 2 + 1) * T], a2[:, h * DK:(h + 1) * DK],
                                        ga1T[:, :], start=True, stop=True)
                    ins.then_inc(sem("gla_pre_psum"), 1)
                for i in range(8):
                    if u == LEVEL_AT + 4 * i + 1:
                        pe.wait_ge(sem("gla_prod"), 2 * (i + 1))
                        if i == 0:
                            pe.wait_ge(sem("gla_pick"), 2)
                            for h in range(H):
                                ins = pe.matmul(mx[:, 0, h * P:(h + 1) * P], g_k[:, h * T:h * T + P],
                                                g_q[:, h * T + P:(h + 1) * T], start=True, stop=True)
                        else:
                            if i > 1:
                                pe.wait_ge(sem("gla_pick"), 2 * i - 1)
                            ins = scores(g_q, g_k, 2 * (i % 2))
                        ins.then_inc(sem("gla_lev_psum"), 1)
                if u == AT_O_A:
                    pe.wait_ge(sem("gla_pick"), 2 + 1 + 14)
                    pe.wait_ge(sem("in_out"), 8)
                    attend(GV, False).then_inc(sem("gla_o"), 1)
                if u == AT_OT_A:
                    pe.wait_ge(sem("gla_out"), NB * H)
                    mixed_transposed((0, 1, 2), (GG, GG + T, GG + 2 * T))
                if u == AT_IF:
                    pe.wait_ge(sem("in_out"), 16)
                    pe.wait_ge(sem("gla_out"), NB * H)
                    for s, c0 in enumerate((MI, MF)):
                        for b in range(NB):
                            ins = transpose(mx[0:H, 3, s * T + b * P:s * T + (b + 1) * P], tok[:, b, c0:c0 + H], P)
                    ins.then_inc(sem("ml_if_psum"), 1)
                if u == AT_RAW:
                    pe.wait_ge(sem("mix_lo"), MIXED_A)
                    pe.wait_ge(sem("ml_abs"), 1)
                    heads_transposed(MQ, MK, sem("ml_raw_psum"))
                if u == AT_MIXED:
                    pe.wait_ge(sem("sgu_v"), NB)
                    pe.wait_ge(sem("ml_q_raw"), 1)
                    for b in range(NB):
                        for h in range(H):
                            ins = pe.matmul(mx[:, b, h * P:(h + 1) * P], sguT[:, h, :], tok[:, b, h * P:(h + 1) * P],
                                            start=True, stop=True)
                    ins.then_inc(sem("sgu_psum"), 1)
                if u == AT_MB:
                    pe.wait_ge(sem("ml_m"), 1)
                    pe.wait_ge(sem("sgu_out"), NB * H)
                    pe.wait_ge(sem("ml_k_raw"), 1)
                    for s, row in enumerate((5, 1)):
                        for b in range(NB):
                            transpose(mx[:, 0, s * 8 + b * H:s * 8 + (b + 1) * H], gates[:, row, b * P:(b + 1) * P], H)
                    for h in range(H):
                        ins = pe.matmul(mx[:, 2 + h // 2, (h % 2) * T:(h % 2 + 1) * T], sel[:, h, :], gates[:, 3, :],
                                        start=True, stop=True)
                    ins.then_inc(sem("ml_mb_psum"), 1)
                if u == AT_OT_C:
                    pe.wait_ge(sem("sgu_out"), NB * H)
                    pe.wait_ge(sem("ml_dif"), 1)
                    mixed_transposed((0, 1), (MQ, MQ + T))
                if u == AT_SC:
                    pe.wait_ge(sem("ml_qk"), 2)
                    pe.wait_ge(sem("ml_dif"), 2 * H + 1)
                    pe.wait_ge(sem("mix_lo"), MIXED_C)
                    for h in range(H):
                        pe.matmul(mx[:, 2 + h // 2, (h % 2) * T:(h % 2 + 1) * T], kTf[:, h * T:h * T + P],
                                  qTf[:, h * T:(h + 1) * T], start=True, stop=True)
                    for h in range(H):
                        ins = pe.matmul(mx[:, 1, h * P:(h + 1) * P], kTf[:, h * T + P:(h + 1) * T],
                                        qTf[:, h * T + P:(h + 1) * T], start=True, stop=True)
                    ins.then_inc(sem("ml_sc_psum"), 1)
                if u == AT_O_B:
                    pe.wait_ge(sem("ml_scored"), 2)
                    pe.wait_ge(sem("in_out"), 22)
                    attend(MV, True).then_inc(sem("ml_o"), 1)
                if u == AT_OT_B:
                    pe.wait_ge(sem("ml_out"), NB * H)
                    mixed_transposed((0, 1, 2), (MO, MO + T, MO + 2 * T))
                for n in range(NG_OUT - 1):
                    if u == OUT_T_AT[n]:
                        x1_transposed(n)
            x1_transposed(NG_OUT - 1)
            pe.wait_ge(sem("h2T_lo_ready"), KC)

            def act_transposed(ready, banks_read=None):
                pe.wait_ge(sem("act_ready"), ready)
                if banks_read is not None:
                    pe.wait_ge(sem("act_lo"), banks_read)
                for i in range(4):
                    for b in range(NB):
                        ins = transpose(mx[:, i // 2, (i % 2) * T + b * P:(i % 2) * T + (b + 1) * P],
                                        act_tok[:, b, i * P:(i + 1) * P], P)
                ins.then_inc(sem("actT_psum"), 1)

            def gate_up(j, peeled, after_first=False):
                for k in range(2 * UPG):
                    if k == 0 and not peeled:
                        pe.wait_ge(sem("gate_used"), j * 2)
                    if k == UPG and not peeled:
                        pe.wait_ge(sem("act_ready"), j * 2)
                    unit(j * (2 * UPG) + (U_FF + k), k % R, GW, hT_hi, hT_lo, UC * (k % UPG), 2 * (k // UPG),
                         k % UPG == 0, k % UPG == UPG - 1)
                    if k == 5 and not peeled:
                        act_transposed(j * 2, None if after_first else j - 1)

            gate_up(0, True)
            gate_up(1, False, True)
            with pe.Fori(2, NG_FF) as j:
                gate_up(j, False)
            act_transposed(2 * NG_FF, NG_FF - 1)

            pe.wait_ge(sem("act_lo"), NG_FF)
            with pe.Fori(0, NG_DN // 2) as i:
                for k in range(2 * UPD):
                    if k == 0:
                        pe.wait_ge(sem("residual_added"), i * 4 + 2 * NG_OUT)
                    unit(i * (2 * UPD) + (U_DN + k), k % R, GW, actT_hi, actT_lo, UC * (k % UPD), 2 * (k // UPD),
                         k % UPD == 0, k % UPD == UPD - 1)


_INS = ['x', 'norm_mix', 'w_in', 'gla_a2', 'gla_ab', 'gla_norm', 'ml_conv', 'ml_ib', 'ml_fb', 'ml_norm',
        'sgu_ln_g', 'sgu_ln_b', 'sgu_w', 'sgu_b', 'w_out', 'norm_ffn', 'w_gu', 'w_down', 'norm_final']


def kernel(**inputs):
    import concourse.bacc as bacc
    import numpy as np
    from concourse.bass_utils import run_bass_kernel_spmd

    nc = bacc.Bacc("TRN2", target_bir_lowering=False, num_devices=1)
    arrays, args = {}, []
    for name in _INS:
        a = np.ascontiguousarray(inputs[name])
        if name != 'norm_final':
            a = a[0]
        arrays[f"in_{name}"] = a
        args.append(nc.dram_tensor(f"in_{name}", a.shape, mybir.dt.from_np(a.dtype), kind="ExternalInput").ap())
    out = nc.dram_tensor("y", (T, D), F32, kind="ExternalOutput").ap()
    hybrid_layer(nc, *args, out)
    result = run_bass_kernel_spmd(nc, [arrays], core_ids=[0])
    return result.results[0]["y"].reshape(1, T, D)
```

```python
from contextlib import ExitStack

import concourse.bass as bass
from concourse import mybir

F32 = mybir.dt.float32
F32R = mybir.dt.float32r
I8 = mybir.dt.int8
ALU = mybir.AluOpType
ACT = mybir.ActivationFunctionType
AX_X = mybir.AxisListType.X

P = 128
D = 2048
T = 256
NB = T // P
H = 4
DV = 192
DK = 96
AW = H * DV
CW = D - 2 * AW
RANK = 16
TAU = 16.0
FF = 5632
EPS = 1e-6
KC = D // P
FC = FF // P
GW = 512
UC = 2
R = 4
GELU_C1 = 0.044715
GELU_C0 = 0.7978845608028654

GQ, GK, GV, GG, GA1 = 0, 384, 768, 1536, 2304
MQ, MK, MV, MO, MI, MF = 2320, 2704, 3088, 3856, 4624, 4628
SU, SV = 4632, 5144
IN_GROUPS = [(GQ, GW, 0), (GW, GW, GW), (2048, 272, 2048), (1024, GW, 1024), (1536, GW, 1536),
             (MQ, GW, MQ), (MQ + GW, GW, MQ + GW), (MO + GW, 264, MO + GW),
             (SV, GW, 0), (SU, GW, MQ), (MQ + 1024, GW, MQ + 1024), (MO, GW, MO)]
TOKW = 4632
UPG = KC // UC
UPD = FC // UC
NG_IN, NG_OUT, NG_FF, NG_DN = len(IN_GROUPS), D // GW, FF // GW, D // GW
U_OUT = NG_IN * UPG
U_FF = U_OUT + NG_OUT * UPG
U_DN = U_FF + NG_FF * 2 * UPG
MIX_A, MIX_C, MIX_B = [0, 1, 2], [6, 7], [3, 4, 5]
LEVEL_AT, AT_O_A, AT_OT_A = 38, 70, 82
AT_IF, AT_RAW, AT_AM, AT_MB = 66, 74, 78, 87
CONV_AT = [79, 84, 88, 93]
AT_V, AT_U, AT_LN, AT_MIXED, AT_OT_C = 76, 87, (83, 85), 88, 93
AT_TANH, AT_SC, AT_O_B, AT_OT_B, AT_MO = 95, 96, 99, 103, 100
MIXED_A, MIXED_C, MIXED_B = 6, 10, 16
WARM = 8
LAST = R
START_UNITS = [0, 1, 4, 5]
OUT_ORDER = [(n, k) for n in (0, 1) for k in MIX_A + MIX_C] + [(n, k) for n in (0, 1) for k in MIX_B] \
    + [(n, k) for n in (2, 3) for k in range(UPG)]

OUT_DONE = [U_OUT + max(i for i, (m, _k) in enumerate(OUT_ORDER) if m == n) + 1 for n in range(NG_OUT)]
OUT_AT = [112, 116, 123]
OUT_T_AT = [111, 115, 122]


def hybrid_layer(nc, x, norm_mix, w_in, gla_a2, gla_ab, gla_norm, ml_conv, ml_ib, ml_fb, ml_norm,
                 sgu_ln_g, sgu_ln_b, sgu_w, sgu_b, w_out, norm_ffn, w_gu, w_down, norm_final, out):
    ctx = ExitStack()
    with ctx:
        def sb(name, shape, dt=F32, where=None):
            return (where or ctx).enter_context(nc.sbuf_tensor(name, shape, dt))

        sems = {}

        def sem(name):
            if name not in sems:
                sems[name] = ctx.enter_context(nc.semaphore(name))
            return sems[name]

        raw = sb("raw", [P, R, UC * GW])
        w_hi = sb("w_hi", [P, R, UC * GW], F32R)
        w_lo = sb("w_lo", [P, R, UC * GW], F32R)
        hT_hi = sb("hT_hi", [P, KC, T], F32R)
        hT_lo = sb("hT_lo", [P, KC, T], F32R)
        x1 = sb("x1", [P, NB, D])
        ident = sb("ident", [P, P])
        cols = sb("cols", [P, 36])
        stat = sb("stat", [P, 96])
        ss_x, ms_x, rs_x = stat[:, 0:2], stat[:, 2:4], stat[:, 4:6]
        ss_h, ms_h, rs_h = stat[:, 6:14], stat[:, 14:16], stat[:, 16:18]
        half_rs_h, half_rs2_h = stat[:, 18:20], stat[:, 20:22]
        ss_f, ms_f, rs_f = stat[:, 22:30], stat[:, 30:32], stat[:, 32:34]
        ss_a, ms_a, rs_a = stat[:, 34:42], stat[:, 42:50], stat[:, 50:58]
        minus_half = stat[:, 58:66]
        bn_c = stat[:, 66:78]
        mv_c = stat[:, 78:82]
        rs_c = stat[:, 82:84]
        tot_h, tot_f = stat[:, 84:86], stat[:, 86:88]
        stat_b = sb("stat_b", [P, 80])
        aT = stat_b[:, 0:8]
        mT = stat_b[:, 8:16]
        maxT = stat_b[:, 16:24]
        em = stat_b[:, 24:32]
        den = stat_b[:, 32:40]
        rden = stat_b[:, 40:48]
        ss_b, ms_b, rs_b, fac_b = stat_b[:, 48:56], stat_b[:, 56:64], stat_b[:, 64:72], stat_b[:, 72:80]

        early = ExitStack()
        tok = sb("tok", [P, NB, TOKW], where=early)
        mixT_hi = sb("mixT_hi", [P, KC, T], F32R, early)
        mixT_lo = sb("mixT_lo", [P, KC, T], F32R, early)
        qT = sb("qT", [DK, H, T], where=early)
        kT = sb("kT", [DK, H, T], where=early)
        cum = sb("cum", [DK, H, T], where=early)
        gwork = sb("gwork", [DK, 2080 + H * T], where=early)
        scA = sb("scA", [P, H, T], where=early)
        scB = sb("scB", [P, H, P], where=early)
        levels = sb("levels", [P, 8, P], I8, early)
        gates = sb("gates", [H, 6, T], where=early)
        cols96 = sb("cols96", [DK, 36], where=early)
        ib_fb = sb("ib_fb", [H, 2], where=early)
        a2 = sb("a2", [RANK, H * DK], where=early)
        ga1T = sb("ga1T", [RANK, T], where=early)
        ones = sb("ones", [P, T], where=early)
        mixT_rows = scA[:, 0, :]
        early.close()
        late = ExitStack()
        actT_hi = sb("actT_hi", [P, FC, T], F32R, late)
        actT_lo = sb("actT_lo", [P, FC, T], F32R, late)
        gate_s = sb("gate_s", [P, NB, GW], where=late)
        act_tok = sb("act_tok", [P, NB, GW], where=late)
        nf_row = sb("nf_row", [P, D], where=late)
        late.close()

        xin = tok[:, :, :].rearrange("p b n -> p (b n)")[:, 0:NB * D].rearrange("p (b n) -> p b n", b=NB)
        junk = tok[:, :, :].rearrange("p b n -> p (b n)")[:, NB * D:NB * D + D]
        rowsN = tok[:, :, :].rearrange("p b n -> p (b n)")[0:KC, 6200:6328]
        rowsA = mixT_rows[0:KC + H, 0:P]
        rowsB = mixT_rows[0:H + 32, P:P + DK]
        x1f = x1[:, :, :].rearrange("p b n -> p (b n)")
        gn_row, mn_row = x1f[:, 0:AW], x1f[:, AW:2 * AW]
        lng_row, lnb_row = x1f[:, 1536:2048], x1f[:, 2048:2560]
        sguw = x1f[:, 2560:3072].rearrange("p (g s) -> p g s", g=H)
        sguT = x1f[:, 3072:3584].rearrange("p (g s) -> p g s", g=H)
        g_dif = gwork[:, 0:H * T]
        g_q = gwork[:, H * T:H * T + H * T // 2]
        g_tmp = gwork[:, H * T:2 * H * T]
        g_k = gwork[:, 2080:2080 + H * T]
        PAD = T + 4

        def gl_u(b):
            return tok[:, b, GG:GG + GW]

        def gl_v(b):
            return tok[:, b, GV:GV + GW]

        mraw = gwork[:, 0:2 * H * PAD].rearrange("p (g t) -> p g t", g=2 * H)
        cumf = cum[:, :, :].rearrange("p h t -> p (h t)")
        qTf = qT[:, :, :].rearrange("p h t -> p (h t)")
        kTf = kT[:, :, :].rearrange("p h t -> p (h t)")

        acc = ctx.enter_context(nc.psum_tensor("acc", [P, 4, GW], F32))
        mx = ctx.enter_context(nc.psum_tensor("mx", [P, 4, GW], F32))

        loaded = [sem(f"w_loaded{s}") for s in range(R)]
        hi_ready, lo_ready, unit_used = sem("w_hi_ready"), sem("w_lo_ready"), sem("unit_used")

        def weights(w, row0, c0, width):
            return w[row0:row0 + UC * P, bass.ds(c0, width)].rearrange("(k p) n -> p k n", p=P)

        block = ctx.enter_context(nc.Block())

        @block.sync
        def _(sp):
            def load(w, u, slot, row0, c0, width, first=False):
                if not first:
                    sp.wait_ge(lo_ready, u - R + 1)
                sp.dma_start(raw[:, slot, 0:UC * width].rearrange("p (k n) -> p k n", k=UC),
                             weights(w, row0, c0, width)).then_inc(loaded[slot], 16)

            sp.dma_start(rowsN[:, :], norm_mix.rearrange("(c p) -> c p", p=P)).then_inc(sem("norm_loaded"), 16)
            for q in range(4):
                for b in range(NB):
                    sp.dma_start(xin[:, b, q * GW:(q + 1) * GW],
                                 x[b * P:(b + 1) * P, q * GW:(q + 1) * GW]).then_inc(sem(f"x_loaded{b}{q}"), 16)
                c0, width, _at = IN_GROUPS[0]
                load(w_in, q, q, q * UC * P, c0, width, first=True)
            for u in range(R, U_OUT):
                c0, width, _at = IN_GROUPS[u // UPG]
                load(w_in, u, u % R, (u % UPG) * UC * P, c0, width)
            u = U_OUT
            for n, k in OUT_ORDER:
                load(w_out, u, u % R, k * UC * P, n * GW, GW)
                u += 1
            with sp.Fori(0, NG_FF) as j:
                for k in range(2 * UPG):
                    load(w_gu, j * (2 * UPG) + (U_FF + k), k % R, (k % UPG) * UC * P,
                         j * GW + (FF if k >= UPG else 0), GW)
            for n in range(NG_DN):
                for k in range(UPD):
                    u = U_DN + n * UPD + k
                    load(w_down, u, u % R, k * UC * P, n * GW, GW)
            for b in range(NB):
                for q in range(4):
                    sp.wait_ge(sem(f"y{b}_ready"), q + 1)
                    sp.dma_start(out[b * P:(b + 1) * P, q * GW:(q + 1) * GW],
                                 x1[:, b, q * GW:(q + 1) * GW]).then_inc(sem("y_stored"), 16)
            sp.wait_ge(sem("y_stored"), 16 * 4 * NB)

        @block.gpsimd
        def _(pool):
            chain = [0]

            def link(ins):
                chain[0] += 1
                ins.then_inc(sem("pool_chain"), 1)
                pool.wait_ge(sem("pool_chain"), chain[0])

            def rsqrt_mean(dst, tmp, total, n, eps, done):
                link(pool.tensor_scalar(tmp, total, 1.0 / n, eps, ALU.mult, ALU.add))
                pool.tensor_tensor(dst, tmp, minus_half[:, 0:dst.shape[1]], ALU.pow).then_inc(done, 1)

            link(pool.memset(ident[:, :], 0.0))
            pool.affine_select(out=ident[:, :], in_=ident[:, :], compare_op=ALU.not_equal, fill=1.0, base=0,
                               pattern=[[-1, P]], channel_multiplier=1).then_inc(sem("ident_ready"), 1)
            link(pool.memset(minus_half, -0.5))
            pool.wait_ge(sem("x_loaded13"), 16)
            for dst, src in ((rowsA[0:KC, :], norm_ffn.rearrange("(c p) -> c p", p=P)), (rowsA[KC:KC + H, :], sgu_b),
                             (rowsB[0:H, :], gla_ab.rearrange("(h d) -> h d", d=DK)),
                             (rowsB[H:H + 32, :], ml_conv.rearrange("j (g d) -> (j g) d", d=DK))):
                pool.dma_start(dst, src).then_inc(sem("rows_loaded"), 16)
            pool.dma_start(sguw, sgu_w.rearrange("g t s -> t g s")).then_inc(sem("sguw_loaded"), 16)
            for dst, src in ((a2[:, :], gla_a2), (ib_fb[:, 0:1], ml_ib.rearrange("(h a) -> h a", a=1)),
                             (ib_fb[:, 1:2], ml_fb.rearrange("(h a) -> h a", a=1)),
                             (gn_row, gla_norm.partition_broadcast(P)), (mn_row, ml_norm.partition_broadcast(P)),
                             (lng_row, sgu_ln_g.partition_broadcast(P)), (lnb_row, sgu_ln_b.partition_broadcast(P))):
                pool.dma_start(dst, src).then_inc(sem("small_loaded"), 16)
            pool.memset(ones[:, :], 1.0).then_inc(sem("consts"), 1)
            pool.wait_ge(sem("x_squared"), NB)
            rsqrt_mean(rs_x, ms_x, ss_x, D, EPS, sem("rs_x_ready"))
            link(pool.memset(levels[:, :, :], 1.0))
            for i in range(7):
                half = 64 >> i
                v = levels[:, i, :].rearrange("p (b r) -> p b r", r=2 * half)
                nb = P // (2 * half)
                link(pool.affine_select(out=v, in_=v, compare_op=ALU.is_ge, fill=0.0, base=-half,
                                        pattern=[[0, nb], [1, 2 * half]], channel_multiplier=0))
                link(pool.affine_select(out=v, in_=v, compare_op=ALU.is_ge, fill=0.0, base=0,
                                        pattern=[[-2 * half, nb], [0, 2 * half]], channel_multiplier=1))
                link(pool.affine_select(out=v, in_=v, compare_op=ALU.is_ge, fill=0.0, base=half - 1,
                                        pattern=[[2 * half, nb], [0, 2 * half]], channel_multiplier=-1))
            pool.affine_select(out=levels[:, 7, :], in_=levels[:, 7, :], compare_op=ALU.is_equal, fill=0.0, base=0,
                               pattern=[[-1, P]], channel_multiplier=1).then_inc(sem("consts"), 1)
            pool.wait_ge(sem("rowsT_psum"), 1)
            pool.memset(scA[:, :, :], 0.0).then_inc(sem("consts"), 1)
            pool.memset(scB[:, :, :], 0.0).then_inc(sem("consts"), 1)
            pool.memset(g_k, 0.0).then_inc(sem("consts"), 1)
            pool.wait_ge(sem("sguw_loaded"), 16)
            pool.affine_select(out=sguw, in_=sguw, compare_op=ALU.is_ge, fill=0.0, base=0,
                               pattern=[[0, H], [-1, P]], channel_multiplier=1).then_inc(sem("sguw_tril"), 1)

            pool.wait_ge(sem("gla_squared"), NB * H)
            rsqrt_mean(rs_a, ms_a, ss_a, DV, EPS, sem("rs_a_ready"))
            pool.wait_ge(sem("bn_ready"), NB)
            rsqrt_mean(rs_c, mv_c.rearrange("p (b k) -> p b k", b=NB)[:, :, 1],
                       mv_c.rearrange("p (b k) -> p b k", b=NB)[:, :, 1], 1, 4 * EPS, sem("rs_c_ready"))
            pool.wait_ge(sem("ml_exp"), 2)
            pool.affine_select(out=scA[:, :, 0:P], in_=scA[:, :, 0:P], compare_op=ALU.is_ge, fill=0.0, base=0,
                               pattern=[[0, H], [1, P]], channel_multiplier=-1).then_inc(sem("ml_causal"), 1)
            pool.affine_select(out=scB[:, :, :], in_=scB[:, :, :], compare_op=ALU.is_ge, fill=0.0, base=0,
                               pattern=[[0, H], [1, P]], channel_multiplier=-1).then_inc(sem("ml_causal"), 1)
            pool.wait_ge(sem("ms_b_ready"), 1)
            rsqrt_mean(rs_b, ms_b, ms_b, 1, EPS, sem("rs_b_ready"))
            pool.wait_ge(sem("mix_lo"), MIXED_B)
            for b in range(NB):
                pool.dma_start(x1[:, b, :], x[b * P:(b + 1) * P, :]).then_inc(sem("x_again"), 16)
            pool.wait_ge(sem("tot_h_ready"), 1)
            rsqrt_mean(rs_h, ms_h, tot_h, D, EPS, sem("rs_h_ready"))
            pool.wait_ge(unit_used, U_FF)
            pool.dma_start(nf_row[:, :], norm_final.partition_broadcast(P)).then_inc(sem("nf_loaded"), 16)
            for b in range(NB):
                pool.wait_ge(sem("tot_f_ready"), b + 1)
                rsqrt_mean(rs_f[:, b:b + 1], ms_f[:, b:b + 1], tot_f[:, b:b + 1], D, EPS, sem("rs_f_ready"))

        @block.scalar
        def _(act):
            act.wait_ge(sem("ident_ready"), 1)
            act.activation(stat[:, 88:89], ident[:, 0:1], ACT.Copy).then_inc(sem("table_warm"), 1)

            def high(u, slot, width, uses, fresh=False):
                act.wait_ge(loaded[slot], uses)
                if not fresh:
                    act.wait_ge(unit_used, u - R + 1)
                act.activation(w_hi[:, slot, 0:UC * width], raw[:, slot, 0:UC * width], ACT.Copy)\
                   .then_inc(hi_ready, 1)

            def transposed_high(bank, c, dst, scale, done):
                for i in range(2):
                    act.activation(dst[:, c + i, :], mx[:, bank, i * T:(i + 1) * T], ACT.Copy, scale=scale(c + i))\
                       .then_inc(done, 1)

            def mix_high(batch, bank, c):
                act.wait_ge(sem("mixT_psum"), batch + 1)
                transposed_high(bank, c, mixT_hi, lambda _c: 0.5, sem("mix_hi"))

            def evacuate(g):
                _c0, width, at = IN_GROUPS[g]
                act.wait_ge(unit_used, (g + 1) * UPG)
                if g == 0:
                    act.wait_ge(sem("rs_x_ready"), 1)
                    act.wait_ge(sem("hT_lo_ready"), KC)
                if g == 8:
                    act.wait_ge(sem("gla_gate"), NB)
                if g == 9:
                    act.wait_ge(sem("ml_raw_psum"), 1)
                for b in range(NB):
                    act.activation(tok[:, b, at:at + width], acc[:, (g % 2) * 2 + b, 0:width], ACT.Copy,
                                   scale=rs_x[:, b:b + 1]).then_inc(sem("in_out"), 1)

            def softplus(buf, done):
                act.activation(buf, buf, ACT.Exp, scale=-1.0).then_inc(done, 1)
                act.wait_ge(done, 1)
                act.activation(buf, buf, ACT.Ln, bias=1.0).then_inc(done, 1)

            def squares(start, v0, ss, done):
                act.wait_ge(start, 1)
                for b in range(NB):
                    for h in range(H):
                        act.activation(tok[:, b, v0 + h * DV:v0 + (h + 1) * DV],
                                       mx[:, 2 * b + h // 2, (h % 2) * DV:(h % 2 + 1) * DV], ACT.Square,
                                       accum_out=ss[:, b * H + h:b * H + h + 1]).then_inc(done, 1)

            def out_squares(n):
                for b in range(NB):
                    act.wait_ge(sem("residual_added"), 2 * n + b + 1)
                    act.activation(scA[:, 0:2, :].rearrange("p h t -> p (h t)"), x1[:, b, n * GW:(n + 1) * GW],
                                   ACT.Square, accum_out=ss_h[:, b * NG_OUT + n:b * NG_OUT + n + 1])\
                       .then_inc(sem("h_squared"), 1)
                    act.wait_ge(sem("h_squared"), 2 * n + b + 1)

            def out_high(n):
                act.wait_ge(sem("x1T_psum"), n + 1)
                for i in range(2):
                    transposed_high((n % 2) * 2 + i, 4 * n + 2 * i, hT_hi, lambda c: cols[:, KC + c:KC + c + 1],
                                    sem("h2T_hi_ready"))

            act.wait_ge(sem("cols_ready"), 1)
            for b in range(KC // 2):
                act.wait_ge(sem("xT_psum"), b + 1)
                transposed_high(b % 4, 2 * b, hT_hi, lambda c: cols[:, c:c + 1], sem("hT_hi_ready"))
                if b in START_UNITS:
                    k = START_UNITS.index(b)
                    high(k, k, GW, 16, fresh=True)

            for u in range(R, U_FF):
                g = u // UPG
                high(u, u % R, IN_GROUPS[g][1] if g < NG_IN else GW, 16 * (u // R + 1))
                if u % UPG == 3 and 1 <= g <= NG_IN:
                    evacuate(g - 1)
                if u in (5, 6):
                    b = u - 5
                    act.activation(junk, xin[:, b, :], ACT.Square, accum_out=ss_x[:, b:b + 1])\
                       .then_inc(sem("x_squared"), 1)
                    act.wait_ge(sem("x_squared"), b + 1)
                if u == 19:
                    act.wait_ge(sem("sguT_psum"), 1)
                    act.activation(sguT, mx[:, 3, :].rearrange("p (g s) -> p g s", g=H), ACT.Copy)\
                       .then_inc(sem("sguT_ready"), 1)
                if u == 23:
                    act.wait_ge(sem("gla_qk_psum"), 1)
                    act.activation(qTf, mx[0:DK, 0:2, :].rearrange("p k n -> p (k n)"), ACT.Copy,
                                   scale=DK ** -0.5).then_inc(sem("gla_qT"), 1)
                if u == 36:
                    act.wait_ge(sem("gla_abs"), 1)
                    softplus(g_dif, sem("gla_sp"))
                for i in range(8):
                    if u == LEVEL_AT + 4 * i:
                        act.wait_ge(sem("gla_dif"), 2 * (i + 1))
                        act.activation(g_dif, g_dif, ACT.Exp, scale=1.0 / TAU).then_inc(sem("gla_decay"), 1)
                if u == 45:
                    act.wait_ge(sem("in_out"), 2 * 5)
                    act.wait_ge(sem("gla_qk_psum"), 1)
                    for b in range(NB):
                        act.activation(tok[:, b, 0:AW], tok[:, b, GG:GG + AW], ACT.Tanh, scale=0.5)\
                           .then_inc(sem("gla_tanh"), 1)
                if u == AT_O_A + 4:
                    squares(sem("gla_o"), GV, ss_a, sem("gla_squared"))
                if u == AT_OT_A + 4:
                    for i in range(3):
                        mix_high(i, i, 2 * i)
                if u == AT_IF + 4:
                    act.wait_ge(sem("ml_abs"), 1)
                    softplus(gates[:, 3, :], sem("ml_sp"))
                if u == AT_RAW + 4:
                    act.wait_ge(sem("ml_raw_psum"), 1)
                    act.wait_ge(sem("ml_pad"), 1)
                    act.activation(mraw[:, 0:H, 3:3 + T], mx[0:DK, 0:2, :].rearrange("p k (h t) -> p (k h) t", t=T),
                                   ACT.Copy).then_inc(sem("ml_q_raw"), 1)
                if u == AT_MB + 4:
                    act.wait_ge(sem("ml_dif"), 2 * H)
                    act.wait_ge(sem("ml_am"), 1)
                    act.activation(scA[:, :, :], scA[:, :, :], ACT.Exp, scale=-1.0).then_inc(sem("ml_exp"), 1)
                    act.activation(scB[:, :, :], scB[:, :, :], ACT.Exp, scale=-1.0).then_inc(sem("ml_exp"), 1)
                    act.activation(em, mT, ACT.Exp, scale=-1.0).then_inc(sem("ml_em"), 1)
                if u == AT_TANH:
                    act.wait_ge(sem("ml_conv_done"), 8)
                    act.activation(gwork[:, 0:H * T], qTf, ACT.Tanh, scale=0.5).then_inc(sem("ml_tanh"), 1)
                    act.activation(gwork[:, H * T:2 * H * T], kTf, ACT.Tanh, scale=0.5).then_inc(sem("ml_tanh"), 1)
                for at, n_in, buf, col, name in ((AT_V, 18, gl_v, 0, "v"), (AT_U, 20, gl_u, MQ, "u")):
                    if u == at:
                        act.wait_ge(sem("in_out"), n_in)
                        act.wait_ge(sem("gla_squared"), NB * H)
                        if name == "u":
                            act.wait_ge(sem("mixT_psum"), 3)
                        for b in range(NB):
                            act.activation(buf(b), tok[:, b, col:col + GW], ACT.Square)\
                               .then_inc(sem(f"gelu_sq_{name}"), 1)
                    for b in range(NB):
                        if u == at + 3 + b:
                            act.wait_ge(sem(f"gelu_arg_{name}"), b + 1)
                            act.activation(buf(b), buf(b), ACT.Tanh, scale=GELU_C0).then_inc(sem(f"gelu_tanh_{name}"), 1)
                if u == AT_OT_C + 4:
                    mix_high(3, 0, 12)
                    mix_high(4, 1, 14)
                if u == AT_MO:
                    act.wait_ge(sem("in_out"), 2 * NG_IN)
                    act.wait_ge(sem("mixT_psum"), 5)
                    for b in range(NB):
                        act.activation(tok[:, b, MQ:MQ + AW], tok[:, b, MO:MO + AW], ACT.Tanh, scale=0.5)\
                           .then_inc(sem("ml_gate_tanh"), 1)
                if u == AT_O_B + 3:
                    act.wait_ge(sem("ml_o"), 1)
                    act.activation(den.rearrange("p (k h) -> p k h", h=2), mx[:, :, 2 * DV:2 * DV + 2], ACT.Copy)\
                       .then_inc(sem("ml_den"), 1)
                    squares(sem("ml_o"), MV, ss_b, sem("ml_squared"))
                if u == AT_OT_B + 4:
                    for i in range(3):
                        mix_high(5 + i, i, 6 + 2 * i)
                for n in range(NG_OUT - 1):
                    if u == OUT_AT[n]:
                        out_squares(n)
                    if u == OUT_T_AT[n] + 4:
                        out_high(n)
            def gate_tanh(used, gates_read=None):
                act.wait_ge(unit_used, used)
                if gates_read is not None:
                    act.wait_ge(sem("act_ready"), gates_read)
                for b in range(NB):
                    act.activation(gate_s[:, b, :], acc[:, b, :], ACT.Tanh, scale=half_rs_h[:, b:b + 1])\
                       .then_inc(sem("gate_tanh"), 1)

            def act_high(groups, c):
                act.wait_ge(sem("actT_psum"), groups)
                act.activation(actT_hi[:, bass.ds(c, 4), :].rearrange("p c t -> p (c t)"),
                               mx[:, 0:2, :].rearrange("p k n -> p (k n)"), ACT.Copy).then_inc(sem("act_hi"), 1)

            def gate_up(j, peeled):
                for k in range(2 * UPG):
                    high(j * (2 * UPG) + (U_FF + k), k % R, GW, j * (16 * 2 * UPG // R) + 16 * ((U_FF + k) // R + 1))
                    if peeled and k == 3:
                        out_squares(NG_OUT - 1)
                    if peeled and k == 6:
                        out_high(NG_OUT - 1)
                    if k == 9 and not peeled:
                        act_high(j, j * 4 - 4)
                    if k == 11:
                        if peeled:
                            act.wait_ge(sem("rs_h2_ready"), 1)
                        gate_tanh(j * (2 * UPG) + (U_FF + UPG), None if peeled else j * 2)

            gate_up(0, True)
            with act.Fori(1, NG_FF) as j:
                gate_up(j, False)
            def down_squares(n):
                for b in range(NB):
                    act.wait_ge(sem("residual_added"), 2 * NG_OUT + 2 * n + b + 1)
                    act.activation(gate_s[:, 0, :], x1[:, b, n * GW:(n + 1) * GW], ACT.Square,
                                   accum_out=ss_f[:, b * NG_DN + n:b * NG_DN + n + 1]).then_inc(sem("f_squared"), 1)
                    act.wait_ge(sem("f_squared"), 2 * n + b + 1)

            for n in range(NG_DN):
                for k in range(UPD):
                    u = U_DN + n * UPD + k
                    high(u, u % R, GW, 16 * (u // R + 1))
                    if n == 0 and k == 9:
                        act_high(NG_FF, 4 * (NG_FF - 1))
                    if n > 0 and k == 4:
                        down_squares(n - 1)
            down_squares(NG_DN - 1)
            act.wait_ge(sem("rs_f_ready"), 2)
            for q in range(4):
                y = x1[:, 1, q * GW:(q + 1) * GW]
                if q == NG_DN - 1:
                    act.wait_ge(sem("nf_times"), 2 * NG_DN)
                act.activation(y, y, ACT.Copy, scale=rs_f[:, 1:2]).then_inc(sem("y1_ready"), 1)

        @block.vector
        def _(dve):
            chain = [0]

            def step(ins):
                chain[0] += 1
                ins.then_inc(sem("dve_chain"), 1)

            def settle():
                dve.wait_ge(sem("dve_chain"), chain[0])

            def low(u, slot, width):
                dve.wait_ge(hi_ready, u + 1)
                dve.tensor_tensor(w_lo[:, slot, 0:UC * width], raw[:, slot, 0:UC * width],
                                  w_hi[:, slot, 0:UC * width].bitcast(F32), ALU.subtract).then_inc(lo_ready, 1)

            def transposed_low(bank, c, hi, lo, scale, done):
                for i in range(2):
                    dve.scalar_tensor_tensor(out=lo[:, c + i, :], in0=mx[:, bank, i * T:(i + 1) * T], scalar=scale(c + i),
                                             in1=hi[:, c + i, :].bitcast(F32), op0=ALU.mult, op1=ALU.subtract)\
                       .then_inc(done, 1)

            def mix_low(batch, bank, c):
                dve.wait_ge(sem("mix_hi"), 2 * (batch + 1))
                transposed_low(bank, c, mixT_hi, mixT_lo, lambda _c: 0.5, sem("mix_lo"))

            dve.wait_ge(sem("colsT_psum"), 1)
            dve.tensor_copy(cols[:, 0:KC], acc[:, 2, 0:KC]).then_inc(sem("cols_ready"), 1)
            for b in range(KC // 2):
                dve.wait_ge(sem("hT_hi_ready"), 2 * (b + 1))
                transposed_low(b % 4, 2 * b, hT_hi, hT_lo, lambda c: cols[:, c:c + 1], sem("hT_lo_ready"))
                if b in START_UNITS:
                    k = START_UNITS.index(b)
                    low(k, k, GW)

            def gla_logsig():
                dve.wait_ge(sem("gla_pre_psum"), 1)
                dve.wait_ge(sem("rowsT_read"), 2)
                for h in range(H):
                    step(dve.tensor_scalar(cum[:, h, :], mx[0:DK, 2 + h // 2, (h % 2) * T:(h % 2 + 1) * T],
                                           cols96[:, h:h + 1], None, ALU.add))
                settle()
                step(dve.tensor_scalar(g_tmp, cumf, 0.0, None, ALU.min))
                settle()
                dve.scalar_tensor_tensor(out=g_dif, in0=g_tmp, scalar=-2.0, in1=cumf, op0=ALU.mult, op1=ALU.add)\
                   .then_inc(sem("gla_abs"), 1)

            def gla_cumulate():
                dve.wait_ge(sem("gla_sp"), 2)
                dve.wait_ge(sem("consts"), 5)
                step(dve.tensor_tensor(g_tmp, g_tmp, g_dif, ALU.subtract))
                settle()
                for h in range(H):
                    step(dve.tensor_tensor_scan(cum[:, h, :], ones[0:DK, :], g_tmp[:, h * T:(h + 1) * T], 0.0,
                                                ALU.mult, ALU.add))
                settle()

            def gla_differences(i):
                half = P >> i
                if i == 0:
                    c = cumf.rearrange("p (n a r) -> p n a r", a=2, r=half)
                    d = g_dif.rearrange("p (n a r) -> p n a r", a=2, r=half)
                else:
                    dve.wait_ge(sem("gla_prod"), 2 * i)
                    c = cumf.rearrange("p (n a r) -> p n a r", a=2, r=half)
                    d = g_dif.rearrange("p (n a r) -> p n a r", a=2, r=half)
                n = H * T // (2 * half)
                ref = c[:, :, 0, half - 1:half].to_broadcast([DK, n, half])
                dve.tensor_tensor(d[:, :, 0, :], ref, c[:, :, 0, :], ALU.subtract).then_inc(sem("gla_dif"), 1)
                dve.tensor_tensor(d[:, :, 1, :], c[:, :, 1, :], ref, ALU.subtract).then_inc(sem("gla_dif"), 1)

            def gla_products(i):
                half = P >> i
                dve.wait_ge(sem("gla_decay"), i + 1)
                if i > 0:
                    dve.wait_ge(sem("gla_lev_psum"), i + 1)
                d, q, k, g = (t.rearrange("p (n a r) -> p n a r", a=2, r=half) for t in (g_dif, qTf, kTf, g_k))
                dve.tensor_tensor(g_q.rearrange("p (n r) -> p n r", r=half), q[:, :, 1, :], d[:, :, 1, :], ALU.mult)\
                   .then_inc(sem("gla_prod"), 1)
                dve.tensor_tensor(g[:, :, 0, :], k[:, :, 0, :], d[:, :, 0, :], ALU.mult).then_inc(sem("gla_prod"), 1)

            def gla_pick(i):
                half = P >> i
                for b, dst in enumerate((scA[:, :, 0:P], scB[:, :, :])):
                    upper = dst.rearrange("p h (n a r) -> p h n a r", a=2, r=half)[:, :, :, 1, :]
                    mask = levels[:, i - 1, :].rearrange("p (n a r) -> p n a r", a=2, r=half)[:, :, 1, :]
                    n = P // (2 * half)
                    if n == 1:
                        upper, mask = upper[:, :, 0, :], mask[:, 0, :].unsqueeze(1).to_broadcast([P, H, half])
                        data = mx[:, i % 2, b * T:(b + 1) * T].rearrange("p (h r) -> p h r", h=H)
                    else:
                        mask = mask.unsqueeze(1).to_broadcast([P, H, n, half])
                        data = mx[:, i % 2, b * T:(b + 1) * T].rearrange("p (h n r) -> p h n r", h=H, r=half)
                    dve.copy_predicated(upper, mask, data).then_inc(sem("gla_pick"), 1)

            def out_add(n):
                dve.wait_ge(unit_used, OUT_DONE[n])
                dve.wait_ge(sem("x_again"), 16 * NB)
                for b in range(NB):
                    dst = x1[:, b, n * GW:(n + 1) * GW]
                    dve.tensor_tensor(dst, acc[:, 2 * (n % 2) + b, :], dst, ALU.add).then_inc(sem("residual_added"), 1)

            def out_low(n):
                for i in range(2):
                    dve.wait_ge(sem("h2T_hi_ready"), 4 * n + 2 * i + 2)
                    transposed_low((n % 2) * 2 + i, 4 * n + 2 * i, hT_hi, hT_lo, lambda c: cols[:, KC + c:KC + c + 1],
                                   sem("h2T_lo_ready"))

            for u in range(R, U_FF):
                g = u // UPG
                low(u, u % R, IN_GROUPS[g][1] if g < NG_IN else GW)
                if u == 13:
                    dve.wait_ge(sem("rowsT_psum"), 1)
                    dve.tensor_copy(cols[:, KC:2 * KC + H], mx[:, 0, 0:KC + H]).then_inc(sem("rowsT_read"), 1)
                    dve.tensor_copy(cols96[:, :], mx[0:DK, 1, 0:H + 32]).then_inc(sem("rowsT_read"), 1)
                if u == 23:
                    dve.wait_ge(sem("gla_qk_psum"), 1)
                    dve.tensor_copy(kTf, mx[0:DK, 2:4, :].rearrange("p k n -> p (k n)")).then_inc(sem("gla_kT"), 1)
                if u == 28:
                    dve.wait_ge(sem("gla_lev_psum"), 1)
                    dve.wait_ge(sem("consts"), 5)
                    for b, dst in enumerate((scA[:, :, 0:P], scB[:, :, :])):
                        dve.copy_predicated(dst, levels[:, 7, :].unsqueeze(1).to_broadcast([P, H, P]),
                                            mx[:, b, :].rearrange("p (h t) -> p h t", h=H))\
                           .then_inc(sem("gla_pick"), 1)
                if u == 31:
                    dve.wait_ge(sem("ga1T_psum"), 1)
                    dve.tensor_copy(ga1T[:, :], mx[0:RANK, 2, 0:T]).then_inc(sem("ga1T_ready"), 1)
                if u == 35:
                    gla_logsig()
                if u == 37:
                    gla_cumulate()
                for i in range(8):
                    if u == LEVEL_AT + 4 * i:
                        gla_differences(i)
                    if u == LEVEL_AT + 4 * i + 1:
                        gla_products(i)
                    if u == LEVEL_AT + 4 * i + 5:
                        dve.wait_ge(sem("gla_lev_psum"), i + 2)
                        if i == 0:
                            dve.tensor_copy(scA[:, :, P:T], mx[:, 0, :].rearrange("p (h t) -> p h t", h=H))\
                               .then_inc(sem("gla_pick"), 1)
                        else:
                            gla_pick(i)
                if u in (46, 50):
                    b = (u - 46) // 4
                    dve.wait_ge(sem("gla_tanh"), b + 1)
                    dve.wait_ge(sem("small_loaded"), 16 * 7)
                    step(dve.scalar_tensor_tensor(out=tok[:, b, GG:GG + AW], in0=tok[:, b, 0:AW], scalar=1.0,
                                                  in1=tok[:, b, GG:GG + AW], op0=ALU.add, op1=ALU.mult))
                    settle()
                    dve.tensor_tensor(tok[:, b, GG:GG + AW], tok[:, b, GG:GG + AW], gn_row, ALU.mult)\
                       .then_inc(sem("gla_gate"), 1)
                if u == AT_O_A + 5:
                    dve.wait_ge(sem("rs_a_ready"), 1)
                    dve.wait_ge(sem("gla_gate"), NB)
                    for b in range(NB):
                        for h in range(H):
                            dst = tok[:, b, GG + h * DV:GG + (h + 1) * DV]
                            dve.scalar_tensor_tensor(out=dst, in0=mx[:, 2 * b + h // 2, (h % 2) * DV:(h % 2 + 1) * DV],
                                                     scalar=rs_a[:, b * H + h:b * H + h + 1], in1=dst,
                                                     op0=ALU.mult, op1=ALU.mult).then_inc(sem("gla_out"), 1)
                if u == AT_OT_A + 4:
                    for i in range(3):
                        mix_low(i, i, 2 * i)
                if u == AT_IF + 4:
                    dve.wait_ge(sem("ml_if_psum"), 1)
                    step(dve.tensor_scalar(gates[:, 0, :], mx[0:H, 3, 0:T], ib_fb[:, 0:1], None, ALU.add))
                    step(dve.tensor_scalar(gates[:, 1, :], mx[0:H, 3, T:2 * T], ib_fb[:, 1:2], None, ALU.add))
                    settle()
                    step(dve.tensor_scalar(gates[:, 2, :], gates[:, 1, :], 0.0, None, ALU.min))
                    settle()
                    dve.scalar_tensor_tensor(out=gates[:, 3, :], in0=gates[:, 2, :], scalar=-2.0, in1=gates[:, 1, :],
                                             op0=ALU.mult, op1=ALU.add).then_inc(sem("ml_abs"), 1)
                if u == AT_IF + 5:
                    dve.wait_ge(sem("ml_sp"), 2)
                    step(dve.tensor_tensor(gates[:, 2, :], gates[:, 2, :], gates[:, 3, :], ALU.subtract))
                    settle()
                    step(dve.tensor_tensor_scan(gates[:, 4, :], ones[0:H, :], gates[:, 2, :], 0.0, ALU.mult, ALU.add))
                    settle()
                    step(dve.tensor_tensor(gates[:, 5, :], gates[:, 0, :], gates[:, 4, :], ALU.subtract))
                    settle()
                    step(dve.tensor_tensor_scan(gates[:, 3, :], gates[:, 5, :], gates[:, 5, :], 0.0, ALU.max, ALU.max))
                    settle()
                    dve.tensor_tensor(gates[:, 1, :], gates[:, 4, :], gates[:, 3, :], ALU.add).then_inc(sem("ml_m"), 1)
                if u == AT_RAW + 3:
                    dve.wait_ge(sem("gla_lev_psum"), 9)
                    dve.memset(mraw[:, :, 0:3], 0.0).then_inc(sem("ml_pad"), 1)
                if u == AT_RAW + 4:
                    dve.wait_ge(sem("ml_raw_psum"), 1)
                    dve.tensor_copy(mraw[:, H:2 * H, 3:3 + T], mx[0:DK, 2:4, :].rearrange("p k (h t) -> p (k h) t", t=T))\
                       .then_inc(sem("ml_k_raw"), 1)
                if u in CONV_AT:
                    dve.wait_ge(sem("ml_q_raw"), 1)
                    dve.wait_ge(sem("ml_k_raw"), 1)
                    pair = [(c, (qT if c < H else kT)[:, c % H, :]) for c in (2 * CONV_AT.index(u), 2 * CONV_AT.index(u) + 1)]
                    for c, dst in pair:
                        step(dve.tensor_scalar(dst, mraw[:, c, 0:T], cols96[:, H + c:H + c + 1], None, ALU.mult))
                    for tap in range(1, 4):
                        for c, dst in pair:
                            dve.wait_ge(sem("dve_chain"), chain[0] - 1 if tap < 3 or c % 2 == 0 else chain[0])
                            w = cols96[:, H + 8 * tap + c:H + 8 * tap + c + 1]
                            ins = dve.scalar_tensor_tensor(out=dst, in0=mraw[:, c, tap:tap + T], scalar=w, in1=dst,
                                                           op0=ALU.mult, op1=ALU.add)
                            if tap < 3:
                                step(ins)
                            else:
                                ins.then_inc(sem("ml_conv_done"), 1)
                if u == AT_TANH + 1:
                    for i, t in enumerate((qTf, kTf)):
                        dve.wait_ge(sem("ml_tanh"), i + 1)
                        dve.scalar_tensor_tensor(out=t, in0=gwork[:, i * H * T:(i + 1) * H * T], scalar=1.0, in1=t,
                                                 op0=ALU.add, op1=ALU.mult).then_inc(sem("ml_qk"), 1)
                if u == AT_AM + 4:
                    dve.wait_ge(sem("ml_am_psum"), 1)
                    dve.tensor_copy(stat_b[:, 0:24], mx[:, 3, 0:24]).then_inc(sem("ml_am"), 1)
                if u == AT_MB + 4:
                    dve.wait_ge(sem("ml_mb_psum"), 1)
                    dve.wait_ge(sem("ml_am"), 1)
                    for h in range(H):
                        mb = mx[:, 2 + h // 2, (h % 2) * T:(h % 2 + 1) * T]
                        dve.tensor_scalar(scA[:, h, :], mb, aT[:, h:h + 1], 0.0, ALU.subtract, ALU.max)\
                           .then_inc(sem("ml_dif"), 1)
                        dve.tensor_scalar(scB[:, h, :], mb[:, P:T], aT[:, H + h:H + h + 1], 0.0, ALU.subtract, ALU.max)\
                           .then_inc(sem("ml_dif"), 1)
                for at, buf, col, name in ((AT_V, gl_v, 0, "v"), (AT_U, gl_u, MQ, "u")):
                    for b in range(NB):
                        src = tok[:, b, col:col + GW]
                        if u == at + 1 + b:
                            dve.wait_ge(sem(f"gelu_sq_{name}"), b + 1)
                            step(dve.tensor_scalar(buf(b), buf(b), GELU_C1, 1.0, ALU.mult, ALU.add))
                            settle()
                            dve.tensor_tensor(buf(b), buf(b), src, ALU.mult).then_inc(sem(f"gelu_arg_{name}"), 1)
                        if u == at + 4 + b:
                            dve.wait_ge(sem(f"gelu_tanh_{name}"), b + 1)
                            ins = dve.scalar_tensor_tensor(out=src, in0=buf(b), scalar=1.0, in1=src,
                                                           op0=ALU.add, op1=ALU.mult)
                            if name == "u":
                                ins.then_inc(sem("sgu_u"), 1)
                            else:
                                step(ins)
                                settle()
                                step(dve.bn_stats(out=bn_c[:, 6 * b:6 * b + 6], in_=src))
                                settle()
                                dve.bn_aggr(out=mv_c[:, 2 * b:2 * b + 2], in_=bn_c[:, 6 * b:6 * b + 6])\
                                   .then_inc(sem("bn_ready"), 1)
                for b in range(NB):
                    if u == AT_LN[b]:
                        dve.wait_ge(sem("rs_c_ready"), 1)
                        v = tok[:, b, 0:GW]
                        step(dve.tensor_scalar(v, v, mv_c[:, 2 * b:2 * b + 1], rs_c[:, b:b + 1], ALU.subtract, ALU.mult))
                        settle()
                        step(dve.tensor_tensor(v, v, lng_row, ALU.mult))
                        settle()
                        dve.tensor_tensor(v, v, lnb_row, ALU.add).then_inc(sem("sgu_v"), 1)
                if u == AT_MIXED + 4:
                    dve.wait_ge(sem("sgu_psum"), 1)
                    dve.wait_ge(sem("sgu_u"), NB)
                    for b in range(NB):
                        for h in range(H):
                            dst = tok[:, b, MQ + h * P:MQ + (h + 1) * P]
                            dve.scalar_tensor_tensor(out=dst, in0=mx[:, b, h * P:(h + 1) * P],
                                                     scalar=cols[:, 2 * KC + h:2 * KC + h + 1], in1=dst,
                                                     op0=ALU.add, op1=ALU.mult).then_inc(sem("sgu_out"), 1)
                if u == AT_OT_C + 4:
                    mix_low(3, 0, 12)
                    mix_low(4, 1, 14)
                if u == AT_SC + 3:
                    dve.wait_ge(sem("ml_sc_psum"), 1)
                    dve.wait_ge(sem("ml_causal"), 2)
                    scale = 0.25 * DK ** -0.5
                    for s, src in ((scA[:, :, :], mx[:, 2:4, :].rearrange("p k n -> p (k n)")), (scB[:, :, :], mx[:, 1, :])):
                        s = s.rearrange("p h t -> p (h t)")
                        dve.scalar_tensor_tensor(out=s, in0=src, scalar=scale, in1=s, op0=ALU.mult, op1=ALU.mult)\
                           .then_inc(sem("ml_scored"), 1)
                if u == AT_MO + 2:
                    for b in range(NB):
                        dve.wait_ge(sem("ml_gate_tanh"), b + 1)
                        dve.scalar_tensor_tensor(out=tok[:, b, MO:MO + AW], in0=tok[:, b, MQ:MQ + AW], scalar=1.0,
                                                 in1=mn_row, op0=ALU.add, op1=ALU.mult).then_inc(sem("ml_gate"), 1)
                if u == AT_O_B + 3:
                    dve.wait_ge(sem("ml_den"), 1)
                    dve.wait_ge(sem("ml_em"), 1)
                    step(dve.scalar_tensor_tensor(out=rden, in0=den, scalar=-1.0, in1=den, op0=ALU.mult, op1=ALU.max))
                    settle()
                    step(dve.tensor_tensor(rden, rden, em, ALU.max))
                    settle()
                    step(dve.reciprocal(rden, rden))
                    settle()
                    dve.wait_ge(sem("ml_squared"), NB * H)
                    step(dve.tensor_tensor(ms_b, ss_b, rden, ALU.mult))
                    settle()
                    step(dve.tensor_tensor(ms_b, ms_b, rden, ALU.mult))
                    settle()
                    dve.tensor_scalar(ms_b, ms_b, 1.0 / DV, None, ALU.mult).then_inc(sem("ms_b_ready"), 1)
                if u == AT_O_B + 4:
                    dve.wait_ge(sem("rs_b_ready"), 1)
                    step(dve.tensor_tensor(fac_b, rden, rs_b, ALU.mult))
                    settle()
                    dve.wait_ge(sem("ml_gate"), NB)
                    for b in range(NB):
                        for h in range(H):
                            dst = tok[:, b, MO + h * DV:MO + (h + 1) * DV]
                            dve.scalar_tensor_tensor(out=dst, in0=mx[:, 2 * b + h // 2, (h % 2) * DV:(h % 2 + 1) * DV],
                                                     scalar=fac_b[:, b * H + h:b * H + h + 1], in1=dst,
                                                     op0=ALU.mult, op1=ALU.mult).then_inc(sem("ml_out"), 1)
                if u == AT_OT_B + 4:
                    for i in range(3):
                        mix_low(5 + i, i, 6 + 2 * i)
                for n in range(NG_OUT - 1):
                    if u == OUT_AT[n]:
                        out_add(n)
                    if u == OUT_T_AT[n] + 4:
                        out_low(n)
            def gated(tanhs):
                for b in range(NB):
                    dve.wait_ge(sem("gate_tanh"), tanhs + b + 1)
                    dve.scalar_tensor_tensor(out=gate_s[:, b, :], in0=gate_s[:, b, :], scalar=1.0, in1=acc[:, b, :],
                                             op0=ALU.add, op1=ALU.mult).then_inc(sem("gate_used"), 1)

            def activate(used, gates_done, transposed=None):
                dve.wait_ge(unit_used, used)
                dve.wait_ge(sem("gate_used"), gates_done)
                if transposed is not None:
                    dve.wait_ge(sem("actT_psum"), transposed)
                for b in range(NB):
                    dve.scalar_tensor_tensor(out=act_tok[:, b, :], in0=acc[:, 2 + b, :], scalar=half_rs2_h[:, b:b + 1],
                                             in1=gate_s[:, b, :], op0=ALU.mult, op1=ALU.mult)\
                       .then_inc(sem("act_ready"), 1)

            def act_low(groups, c):
                dve.wait_ge(sem("act_hi"), groups)
                d = bass.ds(c, 4)
                dve.tensor_tensor(actT_lo[:, d, :].rearrange("p c t -> p (c t)"), mx[:, 0:2, :].rearrange("p k n -> p (k n)"),
                                  actT_hi[:, d, :].rearrange("p c t -> p (c t)").bitcast(F32), ALU.subtract)\
                   .then_inc(sem("act_lo"), 1)

            def gate_up(j, peeled, after_first=False):
                for k in range(2 * UPG):
                    low(j * (2 * UPG) + (U_FF + k), k % R, GW)
                    if peeled and k == 3:
                        out_add(NG_OUT - 1)
                    if peeled and k == 6:
                        out_low(NG_OUT - 1)
                        dve.wait_ge(sem("h_squared"), 2 * NG_OUT)
                        dve.tensor_reduce(out=tot_h, in_=ss_h.rearrange("p (b n) -> p b n", b=NB), axis=AX_X,
                                          op=ALU.add).then_inc(sem("tot_h_ready"), 1)
                    if k == 3 and not peeled:
                        activate(j * (2 * UPG) + U_FF, j * 2, None if after_first else j - 1)
                    if k == 9 and not peeled:
                        act_low(j, j * 4 - 4)
                    if k == 11:
                        if peeled:
                            dve.wait_ge(sem("rs_h_ready"), 1)
                            step(dve.tensor_tensor(half_rs2_h, rs_h, rs_h, ALU.mult))
                            dve.tensor_scalar(half_rs_h, rs_h, 0.5, None, ALU.mult).then_inc(sem("rs_h2_ready"), 1)
                            settle()
                            step(dve.tensor_scalar(half_rs2_h, half_rs2_h, 0.5, None, ALU.mult))
                            settle()
                        gated(j * 2)

            gate_up(0, True)
            gate_up(1, False, True)
            with dve.Fori(2, NG_FF) as j:
                gate_up(j, False)
            def down_add(n, b):
                if n == NG_DN - 1 and b == 0:
                    dve.wait_ge(sem("last_block0"), 1)
                else:
                    dve.wait_ge(unit_used, U_DN + (n + 1) * UPD)
                dst = x1[:, b, n * GW:(n + 1) * GW]
                dve.tensor_tensor(dst, acc[:, 2 * (n % 2) + b, :], dst, ALU.add).then_inc(sem("residual_added"), 1)

            def norm_row(n, b):
                dve.wait_ge(sem("f_squared"), 2 * n + b + 1)
                dve.wait_ge(sem("nf_loaded"), 16)
                y = x1[:, b, n * GW:(n + 1) * GW]
                dve.tensor_tensor(y, y, nf_row[:, n * GW:(n + 1) * GW], ALU.mult).then_inc(sem("nf_times"), 1)

            for n in range(NG_DN):
                for k in range(UPD):
                    u = U_DN + n * UPD + k
                    low(u, u % R, GW)
                    if n == 0 and k == 3:
                        activate(U_DN, 2 * NG_FF, NG_FF - 1)
                    if n == 0 and k == 9:
                        act_low(NG_FF, 4 * (NG_FF - 1))
                    if n > 0 and k == 3:
                        for b in range(NB):
                            down_add(n - 1, b)
                    if n > 0 and k == 7:
                        for b in range(NB):
                            norm_row(n - 1, b)
            for b in range(NB):
                down_add(NG_DN - 1, b)
                dve.wait_ge(sem("f_squared"), 2 * (NG_DN - 1) + b + 1)
                dve.tensor_reduce(out=tot_f[:, b:b + 1], in_=ss_f[:, b * NG_DN:(b + 1) * NG_DN], axis=AX_X, op=ALU.add)\
                   .then_inc(sem("tot_f_ready"), 1)
                norm_row(NG_DN - 1, b)
                if b == 0:
                    dve.wait_ge(sem("nf_times"), 2 * NG_DN - 1)
                    dve.wait_ge(sem("rs_f_ready"), 1)
                    for q in range(4):
                        y = x1[:, 0, q * GW:(q + 1) * GW]
                        dve.tensor_scalar(y, y, rs_f[:, 0:1], None, ALU.mult).then_inc(sem("y0_ready"), 1)

        @block.tensor
        def _(pe):
            def transpose(dst, src, n):
                return pe.transpose(dst, src, ident[0:n, 0:n])

            def unit_block(b, slot, width, hi, lo, c, bank, first, last):
                for i in range(UC):
                    o = acc[:, bank + b, 0:width]
                    tb = slice(b * P, (b + 1) * P)
                    wh, wl = (w[:, slot, i * width:(i + 1) * width] for w in (w_hi, w_lo))
                    pe.matmul(o, hi[:, c + i, tb], wh, start=first and i == 0, stop=False)
                    pe.matmul(o, hi[:, c + i, tb], wl, start=False, stop=False)
                    ins = pe.matmul(o, lo[:, c + i, tb], wh, start=False, stop=last and i == UC - 1)
                return ins

            def unit(u, slot, *rest):
                pe.wait_ge(lo_ready, u + 1)
                for b in range(NB):
                    ins = unit_block(b, slot, *rest)
                ins.then_inc(unit_used, 1)

            def first_unit():
                chunks = [(acc[:, b, 0:GW], i, slice(b * P, (b + 1) * P)) for b in range(NB) for i in range(UC)]
                pe.wait_ge(hi_ready, 1)
                for o, i, tb in chunks:
                    wh = w_hi[:, 0, i * GW:(i + 1) * GW]
                    pe.matmul(o, hT_hi[:, i, tb], wh, start=i == 0, stop=False)
                    pe.matmul(o, hT_lo[:, i, tb], wh, start=False, stop=False)
                pe.wait_ge(lo_ready, 1)
                for o, i, tb in chunks:
                    ins = pe.matmul(o, hT_hi[:, i, tb], w_lo[:, 0, i * GW:(i + 1) * GW], start=False, stop=False)
                ins.then_inc(unit_used, 1)

            pe.wait_ge(sem("ident_ready"), 1)

            def x_transposed(b):
                if b >= 4:
                    pe.wait_ge(sem("hT_lo_ready"), 2 * (b - 3))
                for t in range(NB):
                    if b % 2 == 0:
                        pe.wait_ge(sem(f"x_loaded{t}{b // 2}"), 16)
                    for i in range(2):
                        c = 2 * b + i
                        ins = transpose(mx[:, b % 4, i * T + t * P:i * T + (t + 1) * P], xin[:, t, c * P:(c + 1) * P], P)
                ins.then_inc(sem("xT_psum"), 1)

            for _ in range(WARM):
                pe.matmul(acc[:, 3, 0:P], ident[:, :], ident[:, :], start=True, stop=True)
            pe.wait_ge(sem("norm_loaded"), 16)
            transpose(acc[:, 2, 0:KC], rowsN, KC).then_inc(sem("colsT_psum"), 1)
            for b in range(4):
                x_transposed(b)

            def heads_transposed(q0, k0, done):
                for s, c0 in enumerate((q0, k0)):
                    for h in range(H):
                        for b in range(NB):
                            ins = transpose(mx[0:DK, 2 * s + h // 2, (h % 2) * T + b * P:(h % 2) * T + (b + 1) * P],
                                            tok[:, b, c0 + h * DK:c0 + (h + 1) * DK], P)
                ins.then_inc(done, 1)

            def scores(q, k, bank):
                for b in range(NB):
                    for h in range(H):
                        at = slice(h * T + b * P, h * T + (b + 1) * P)
                        ins = pe.matmul(mx[:, bank + b, h * P:(h + 1) * P], k[:, at], q[:, at], start=True, stop=True)
                return ins

            def attend(v0, with_den):
                for b in range(NB):
                    for h in range(H):
                        bank = 2 * b + h // 2
                        for lo, width, is_den in (((h % 2) * DV, DV, False), (2 * DV + h % 2, 1, True)):
                            if is_den and not with_den:
                                continue
                            o = mx[:, bank, lo:lo + width]
                            terms = [(scA[:, h, b * P:(b + 1) * P], 0)] + ([(scB[:, h, :], 1)] if b else [])
                            for n, (s, kb) in enumerate(terms):
                                v = ones[:, 0:1] if is_den else tok[:, kb, v0 + h * DV:v0 + (h + 1) * DV]
                                ins = pe.matmul(o, s, v, start=n == 0, stop=n == len(terms) - 1)
                return ins

            def mixed_transposed(banks, columns):
                for bank, c0 in zip(banks, columns):
                    for i in range(2):
                        for b in range(NB):
                            ins = transpose(mx[:, bank, i * T + b * P:i * T + (b + 1) * P],
                                            tok[:, b, c0 + i * P:c0 + (i + 1) * P], P)
                    ins.then_inc(sem("mixT_psum"), 1)

            def x1_transposed(n):
                pe.wait_ge(sem("residual_added"), 2 * (n + 1))
                if n < 2:
                    pe.wait_ge(sem("mix_lo"), MIXED_B)
                else:
                    pe.wait_ge(sem("h2T_lo_ready"), 4 * (n - 1))
                for i in range(4):
                    for b in range(NB):
                        c = 4 * n + i
                        ins = transpose(mx[:, (n % 2) * 2 + i // 2, (i % 2) * T + b * P:(i % 2) * T + (b + 1) * P],
                                        x1[:, b, c * P:(c + 1) * P], P)
                ins.then_inc(sem("x1T_psum"), 1)

            for u in range(U_FF):
                g, k = divmod(u, UPG)
                if g < NG_IN:
                    if g == 0:
                        pe.wait_ge(sem("hT_lo_ready"), UC * (k + 1))
                    if g >= 2 and k == 0:
                        pe.wait_ge(sem("in_out"), 2 * (g - 1))
                    if u == 0:
                        first_unit()
                    else:
                        unit(u, u % R, IN_GROUPS[g][1], hT_hi, hT_lo, UC * k, 2 * (g % 2), k == 0, k == UPG - 1)
                else:
                    i = u - U_OUT
                    n, k = OUT_ORDER[i]
                    done = [q for m, q in OUT_ORDER[:i] if m == n]
                    if not done:
                        if n < 2:
                            pe.wait_ge(sem("in_out"), 2 * (NG_IN - 1 + n))
                        else:
                            pe.wait_ge(sem("residual_added"), 2 * (n - 1))
                    pe.wait_ge(sem("mix_lo"), MIXED_A if k in MIX_A else MIXED_C if k in MIX_C else MIXED_B)
                    unit(u, u % R, GW, mixT_hi, mixT_lo, UC * k, 2 * (n % 2), not done, len(done) == UPG - 1)
                if u < 2:
                    x_transposed(4 + 2 * u)
                    x_transposed(5 + 2 * u)
                if u == 9:
                    pe.wait_ge(sem("rows_loaded"), 16 * 4)
                    pe.wait_ge(sem("hT_lo_ready"), KC)
                    transpose(mx[:, 0, 0:KC + H], rowsA, KC + H)
                    transpose(mx[0:DK, 1, 0:H + 32], rowsB, H + 32).then_inc(sem("rowsT_psum"), 1)
                if u == 15:
                    pe.wait_ge(sem("sguw_tril"), 1)
                    pe.wait_ge(sem("rowsT_read"), 2)
                    for h in range(H):
                        ins = transpose(mx[:, 3, h * P:(h + 1) * P], sguw[:, h, :], P)
                    ins.then_inc(sem("sguT_psum"), 1)
                if u == 19:
                    pe.wait_ge(sem("in_out"), 4)
                    pe.wait_ge(sem("sguT_ready"), 1)
                    heads_transposed(GQ, GK, sem("gla_qk_psum"))
                if u == 24:
                    pe.wait_ge(sem("gla_qT"), 1)
                    pe.wait_ge(sem("gla_kT"), 1)
                    scores(qTf, kTf, 0).then_inc(sem("gla_lev_psum"), 1)
                if u == 27:
                    pe.wait_ge(sem("in_out"), 6)
                    for b in range(NB):
                        ins = transpose(mx[0:RANK, 2, b * P:(b + 1) * P], tok[:, b, GA1:GA1 + RANK], P)
                    ins.then_inc(sem("ga1T_psum"), 1)
                if u == 31:
                    pe.wait_ge(sem("ga1T_ready"), 1)
                    pe.wait_ge(sem("small_loaded"), 16 * 7)
                    for h in range(H):
                        ins = pe.matmul(mx[0:DK, 2 + h // 2, (h % 2) * T:(h % 2 + 1) * T], a2[:, h * DK:(h + 1) * DK],
                                        ga1T[:, :], start=True, stop=True)
                    ins.then_inc(sem("gla_pre_psum"), 1)
                for i in range(8):
                    if u == LEVEL_AT + 4 * i + 1:
                        pe.wait_ge(sem("gla_prod"), 2 * (i + 1))
                        if i == 0:
                            pe.wait_ge(sem("gla_pick"), 2)
                            for h in range(H):
                                ins = pe.matmul(mx[:, 0, h * P:(h + 1) * P], g_k[:, h * T:h * T + P],
                                                g_q[:, h * P:(h + 1) * P], start=True, stop=True)
                        else:
                            if i > 1:
                                pe.wait_ge(sem("gla_pick"), 2 * i - 1)
                            for b in range(NB):
                                for h in range(H):
                                    ins = pe.matmul(mx[:, i % 2, b * T + h * 64:b * T + (h + 1) * 64],
                                                    g_k[:, h * T + b * P:h * T + (b + 1) * P],
                                                    g_q[:, h * P + b * 64:h * P + (b + 1) * 64], start=True, stop=True)
                        ins.then_inc(sem("gla_lev_psum"), 1)
                if u == AT_O_A:
                    pe.wait_ge(sem("gla_pick"), 2 + 1 + 14)
                    pe.wait_ge(sem("ml_abs"), 1)
                    pe.wait_ge(sem("in_out"), 8)
                    attend(GV, False).then_inc(sem("gla_o"), 1)
                if u == AT_OT_A:
                    pe.wait_ge(sem("ml_q_raw"), 1)
                    pe.wait_ge(sem("ml_k_raw"), 1)
                    mixed_transposed((0, 1, 2), (GG, GG + T, GG + 2 * T))
                if u == AT_IF:
                    pe.wait_ge(sem("in_out"), 16)
                    for s, c0 in enumerate((MI, MF)):
                        for b in range(NB):
                            ins = transpose(mx[0:H, 3, s * T + b * P:s * T + (b + 1) * P], tok[:, b, c0:c0 + H], P)
                    ins.then_inc(sem("ml_if_psum"), 1)
                if u == AT_RAW:
                    pe.wait_ge(sem("in_out"), 14)
                    pe.wait_ge(sem("gla_out"), NB * H)
                    heads_transposed(MQ, MK, sem("ml_raw_psum"))
                if u == AT_MIXED:
                    pe.wait_ge(sem("sgu_v"), NB)
                    pe.wait_ge(sem("mix_lo"), MIXED_A)
                    for b in range(NB):
                        for h in range(H):
                            ins = pe.matmul(mx[:, b, h * P:(h + 1) * P], sguT[:, h, :], tok[:, b, h * P:(h + 1) * P],
                                            start=True, stop=True)
                    ins.then_inc(sem("sgu_psum"), 1)
                if u == AT_AM:
                    pe.wait_ge(sem("ml_m"), 1)
                    pe.wait_ge(sem("ml_k_raw"), 1)
                    for s, row in enumerate((5, 1, 3)):
                        for b in range(NB):
                            ins = transpose(mx[:, 3, s * 8 + b * H:s * 8 + (b + 1) * H], gates[:, row, b * P:(b + 1) * P], H)
                    ins.then_inc(sem("ml_am_psum"), 1)
                if u == AT_MB:
                    pe.wait_ge(sem("ml_am"), 1)
                    pe.wait_ge(sem("mix_lo"), MIXED_A)
                    for h in range(H):
                        for b in range(NB):
                            at = (h % 2) * T + b * P
                            ins = transpose(mx[:, 2 + h // 2, at:at + P],
                                            maxT[:, b * H + h:b * H + h + 1].to_broadcast([P, P]), P)
                    ins.then_inc(sem("ml_mb_psum"), 1)
                if u == AT_OT_C:
                    pe.wait_ge(sem("sgu_out"), NB * H)
                    mixed_transposed((0, 1), (MQ, MQ + T))
                if u == AT_SC:
                    pe.wait_ge(sem("ml_qk"), 2)
                    pe.wait_ge(sem("ml_dif"), 2 * H)
                    pe.wait_ge(sem("mix_lo"), MIXED_C)
                    for h in range(H):
                        pe.matmul(mx[:, 2 + h // 2, (h % 2) * T:(h % 2 + 1) * T], kTf[:, h * T:h * T + P],
                                  qTf[:, h * T:(h + 1) * T], start=True, stop=True)
                    for h in range(H):
                        ins = pe.matmul(mx[:, 1, h * P:(h + 1) * P], kTf[:, h * T + P:(h + 1) * T],
                                        qTf[:, h * T + P:(h + 1) * T], start=True, stop=True)
                    ins.then_inc(sem("ml_sc_psum"), 1)
                if u == AT_O_B:
                    pe.wait_ge(sem("ml_scored"), 2)
                    pe.wait_ge(sem("in_out"), 22)
                    attend(MV, True).then_inc(sem("ml_o"), 1)
                if u == AT_OT_B:
                    pe.wait_ge(sem("ml_out"), NB * H)
                    mixed_transposed((0, 1, 2), (MO, MO + T, MO + 2 * T))
                for n in range(NG_OUT - 1):
                    if u == OUT_T_AT[n]:
                        x1_transposed(n)
            def act_transposed(ready, banks_read=None):
                pe.wait_ge(sem("act_ready"), ready)
                if banks_read is not None:
                    pe.wait_ge(sem("act_lo"), banks_read)
                for i in range(4):
                    for b in range(NB):
                        ins = transpose(mx[:, i // 2, (i % 2) * T + b * P:(i % 2) * T + (b + 1) * P],
                                        act_tok[:, b, i * P:(i + 1) * P], P)
                ins.then_inc(sem("actT_psum"), 1)

            def gate_up(j, peeled, after_first=False):
                for k in range(2 * UPG):
                    if k == 0 and not peeled:
                        pe.wait_ge(sem("gate_used"), j * 2)
                    if k == UPG and not peeled:
                        pe.wait_ge(sem("act_ready"), j * 2)
                    if peeled:
                        if k == 0:
                            pe.wait_ge(sem("residual_added"), 2 * (NG_OUT - 1))
                        if k == UPG:
                            pe.wait_ge(sem("residual_added"), 2 * NG_OUT)
                        if k < UPG:
                            pe.wait_ge(sem("h2T_lo_ready"), UC * (k + 1))
                    unit(j * (2 * UPG) + (U_FF + k), k % R, GW, hT_hi, hT_lo, UC * (k % UPG), 2 * (k // UPG),
                         k % UPG == 0, k % UPG == UPG - 1)
                    if peeled and k == 2:
                        x1_transposed(NG_OUT - 1)
                    if k == 5 and not peeled:
                        act_transposed(j * 2, None if after_first else j - 1)

            gate_up(0, True)
            gate_up(1, False, True)
            with pe.Fori(2, NG_FF) as j:
                gate_up(j, False)
            for n in range(NG_DN):
                for k in range(UPD - (LAST if n == NG_DN - 1 else 0)):
                    u = U_DN + n * UPD + k
                    if n == 0:
                        pe.wait_ge(sem("act_lo"), min(NG_FF, k // 2 + 1))
                    if n == 0 and k == 0:
                        pe.wait_ge(sem("gate_used"), 2 * NG_FF)
                    if n == 1 and k == 0:
                        pe.wait_ge(sem("act_ready"), 2 * NG_FF)
                    if n > 1 and k == 0:
                        pe.wait_ge(sem("residual_added"), 2 * NG_OUT + 2 * (n - 1))
                    unit(u, u % R, GW, actT_hi, actT_lo, UC * k, 2 * (n % 2), k == 0, k == UPD - 1)
                    if n == 0 and k == 5:
                        act_transposed(2 * NG_FF, NG_FF - 1)
            for b in range(NB):
                for k in range(UPD - LAST, UPD):
                    u = U_DN + (NG_DN - 1) * UPD + k
                    if b == 0:
                        pe.wait_ge(lo_ready, u + 1)
                    ins = unit_block(b, u % R, GW, actT_hi, actT_lo, UC * k, 2 * ((NG_DN - 1) % 2), False, k == UPD - 1)
                    if b == 1:
                        ins.then_inc(unit_used, 1)
                if b == 0:
                    ins.then_inc(sem("last_block0"), 1)


_INS = ['x', 'norm_mix', 'w_in', 'gla_a2', 'gla_ab', 'gla_norm', 'ml_conv', 'ml_ib', 'ml_fb', 'ml_norm',
        'sgu_ln_g', 'sgu_ln_b', 'sgu_w', 'sgu_b', 'w_out', 'norm_ffn', 'w_gu', 'w_down', 'norm_final']


def kernel(**inputs):
    import concourse.bacc as bacc
    import numpy as np
    from concourse.bass_utils import run_bass_kernel_spmd

    nc = bacc.Bacc("TRN2", target_bir_lowering=False, num_devices=1)
    arrays, args = {}, []
    for name in _INS:
        a = np.ascontiguousarray(inputs[name])
        if name != 'norm_final':
            a = a[0]
        arrays[f"in_{name}"] = a
        args.append(nc.dram_tensor(f"in_{name}", a.shape, mybir.dt.from_np(a.dtype), kind="ExternalInput").ap())
    out = nc.dram_tensor("y", (T, D), F32, kind="ExternalOutput").ap()
    hybrid_layer(nc, *args, out)
    result = run_bass_kernel_spmd(nc, [arrays], core_ids=[0])
    return result.results[0]["y"].reshape(1, T, D)
```
